# Optimizing a Trainium2 kernel written in Bass

```python
import jax, jax.numpy as jnp
from jax import lax
import numpy as np

D_MODEL = 1024
BATCH = 1
SEQ = 1024
DEPTH = 1
DEC_BATCH = 8
DEC_SEQ = 1
PAST_LEN = 1024
PAGE_SIZE = 128

A_HEADS = 4
A_DK = 128
A_DV = 128
A_WIDTH = A_HEADS * A_DK
A_CHUNK = 64
B_WIDTH = 512
B_BLOCKS = 8
B_BW = B_WIDTH // B_BLOCKS
CONV_W = 4
LRU_C = 8.0
C_HEADS = 8
C_KV_HEADS = 2
C_GROUP = C_HEADS // C_KV_HEADS
C_DH = 64
C_WIDTH = C_HEADS * C_DH
CMP_LEN = 32
CMP_STRIDE = 16
SLC_BLK = 64
SLC_TOPN = 16
WINDOW = 512
Q_BLK = 128
SLC_QBLK = 32
ROPE_THETA = 10000.0
ATT_SCALE = C_DH ** -0.5
N_BRANCH = 3
BR_WIDTH = 512
C_KV_COLS = 6 * C_KV_HEADS * C_DH
IN_SIZES = (A_WIDTH, A_WIDTH, A_WIDTH, A_WIDTH, B_WIDTH, B_WIDTH, C_WIDTH, C_KV_COLS, 3 * C_HEADS, C_WIDTH, N_BRANCH * D_MODEL)
N_IN = sum(IN_SIZES)
ALPHA = (2 * DEPTH) ** 0.25
BETA = (8 * DEPTH) ** -0.25
LN_EPS = 1e-5
NEG_INF = -1e30
FORCED_SCORE = 1e9

kernel_name = 'hybrid_hgrn2_rglru_nsa_decoder_step'

def layer_norm(x, g, b):
    xf = x.astype(jnp.float32)
    mu = jnp.mean(xf, axis=-1, keepdims=True)
    var = jnp.mean(jnp.square(xf - mu), axis=-1, keepdims=True)
    return ((xf - mu) * lax.rsqrt(var + LN_EPS) * g + b).astype(x.dtype)

def group_rms(o):
    of = o.astype(jnp.float32)
    return of * lax.rsqrt(jnp.mean(of * of, axis=-1, keepdims=True) + LN_EPS)

def rope(x, pos):
    d = x.shape[-1]
    inv = ROPE_THETA ** (-jnp.arange(0, d, 2, dtype=jnp.float32) / d)
    ang = pos.astype(jnp.float32)[:, None] * inv[None, :]
    cos = jnp.cos(ang)[:, None, :]
    sin = jnp.sin(ang)[:, None, :]
    xf = x.astype(jnp.float32)
    x1, x2 = xf[..., : d // 2], xf[..., d // 2:]
    return jnp.concatenate([x1 * cos - x2 * sin, x2 * cos + x1 * sin], axis=-1).astype(x.dtype)

def masked_softmax(s, mask):
    s = jnp.where(mask, s.astype(jnp.float32), NEG_INF)
    return jnp.where(mask, jax.nn.softmax(s, axis=-1), 0.0)

def hgrn2_chunked(q, k, v, log_f, s0):
    B, T, H, DK = q.shape
    n = T // A_CHUNK

    def to_chunks(a):
        return a.reshape(B, n, A_CHUNK, H, a.shape[-1]).transpose(1, 0, 3, 2, 4)

    causal = jnp.tril(jnp.ones((A_CHUNK, A_CHUNK), bool))[:, :, None]

    def step(S, xs):
        qi, ki, vi, gi = xs
        b = jnp.cumsum(gi, axis=2)
        inter = jnp.einsum('bhtk,bhkv->bhtv', qi * jnp.exp(b), S)
        diff = b[:, :, :, None, :] - b[:, :, None, :, :]
        decay = jnp.exp(jnp.where(causal, diff, -jnp.inf))
        att = jnp.sum(qi[:, :, :, None, :] * ki[:, :, None, :, :] * decay, axis=-1)
        intra = jnp.einsum('bhts,bhsv->bhtv', att, vi)
        b_last = b[:, :, -1:, :]
        S_new = jnp.exp(b_last[:, :, 0, :])[..., None] * S + jnp.einsum('bhsk,bhsv->bhkv', ki * jnp.exp(b_last - b), vi)
        return S_new.astype(S.dtype), inter + intra

    S, o = lax.scan(step, s0, (to_chunks(q), to_chunks(k), to_chunks(v), to_chunks(log_f)))
    return o.transpose(1, 0, 3, 2, 4).reshape(B, T, H, -1), S

def hgrn2_recurrent(q, k, v, log_f, s0):
    def step(S, xs):
        qt, kt, vt, gt = xs
        S_new = (jnp.exp(gt)[..., None] * S + kt[..., :, None] * vt[..., None, :]).astype(S.dtype)
        return S_new, jnp.einsum('bhk,bhkv->bhv', qt, S_new)

    S, o = lax.scan(step, s0, (q.swapaxes(0, 1), k.swapaxes(0, 1), v.swapaxes(0, 1), log_f.swapaxes(0, 1)))
    return o.swapaxes(0, 1), S

def _lin_combine(left, right):
    a1, b1 = left
    a2, b2 = right
    return a1 * a2, a2 * b1 + b2

def rglru_branch(xb, z, conv0, h0, conv_w, conv_b, ga_w, ga_b, gx_w, gx_b, lam):
    B, T, W = xb.shape
    xpad = jnp.concatenate([conv0.astype(xb.dtype), xb], axis=1)
    u = conv_b + sum(xpad[:, j:j + T] * conv_w[j] for j in range(CONV_W))
    ub = u.reshape(B, T, B_BLOCKS, B_BW)
    r = jax.nn.sigmoid(jnp.einsum('btnd,nde->btne', ub, ga_w).reshape(B, T, W) + ga_b)
    ig = jax.nn.sigmoid(jnp.einsum('btnd,nde->btne', ub, gx_w).reshape(B, T, W) + gx_b)
    log_a = -LRU_C * r.astype(jnp.float32) * jax.nn.softplus(-lam.astype(jnp.float32))
    a = jnp.exp(log_a)
    bterm = jnp.sqrt(-jnp.expm1(2.0 * log_a)) * (ig * u).astype(jnp.float32)
    bterm = bterm.at[:, 0].add(a[:, 0] * h0.astype(jnp.float32))
    _, hs = lax.associative_scan(_lin_combine, (a, bterm), axis=1)
    y = hs.astype(xb.dtype) * jax.nn.silu(z)
    return y, hs[:, -1].astype(h0.dtype), xpad[:, T:]

def compress(kv_raw, pos_emb, w1, w2):
    B, L = kv_raw.shape[:2]
    n_cmp = (L - CMP_LEN) // CMP_STRIDE + 1
    idx = jnp.arange(n_cmp)[:, None] * CMP_STRIDE + jnp.arange(CMP_LEN)[None, :]
    blk = kv_raw[:, idx] + pos_emb.transpose(1, 0, 2)[None, None, :, :, None, :]
    blk = blk.transpose(0, 1, 3, 4, 2, 5).reshape(B, n_cmp, 2, C_KV_HEADS, CMP_LEN * C_DH)
    hid = jax.nn.gelu(jnp.einsum('bnchi,cio->bncho', blk, w1))
    out = jnp.einsum('bncho,cop->bnchp', hid, w2)
    return out[:, :, 0], out[:, :, 1]

def cmp_attention(q, pos, kc, vc):
    B, Tq = q.shape[:2]
    qg = q.reshape(B, Tq, C_KV_HEADS, C_GROUP, C_DH)
    s = jnp.einsum('btghd,bcgd->bghtc', qg, kc) * ATT_SCALE
    n_cmp = kc.shape[1]
    end = jnp.arange(n_cmp) * CMP_STRIDE + CMP_LEN - 1
    p = masked_softmax(s, end[None, :] <= pos[:, None])
    o = jnp.einsum('bghtc,bcgd->btghd', p.astype(vc.dtype), vc)
    return o.reshape(B, Tq, C_HEADS, C_DH), p

def select_blocks(p_cmp, pos, n_slc):
    n_cmp = p_cmp.shape[-1]
    cs = jnp.arange(n_cmp) * CMP_STRIDE
    ss = jnp.arange(n_slc) * SLC_BLK
    overlap = ((cs[:, None] < ss[None, :] + SLC_BLK) & (cs[:, None] + CMP_LEN > ss[None, :])).astype(jnp.float32)
    imp = jnp.einsum('bghtc,cj->bgtj', p_cmp, overlap)
    cur = pos // SLC_BLK
    j = jnp.arange(n_slc)[None, :]
    valid = j <= cur[:, None]
    forced = (j == 0) | (j == cur[:, None]) | (j == cur[:, None] - 1)
    score = jnp.where(forced, FORCED_SCORE, jnp.where(valid, imp, -1.0))
    _, idx = lax.top_k(score, min(SLC_TOPN, n_slc))
    return idx

def to_blocks(k, n_slc):
    B, L = k.shape[:2]
    kp = jnp.pad(k, ((0, 0), (0, n_slc * SLC_BLK - L), (0, 0), (0, 0)))
    return kp.reshape(B, n_slc, SLC_BLK, C_KV_HEADS, C_DH).transpose(0, 3, 1, 2, 4)

def slc_attention(q, pos, idx, ks_blk, vs_blk):
    B, Tq = q.shape[:2]
    bi = jnp.arange(B)[:, None, None, None]
    gi = jnp.arange(C_KV_HEADS)[None, :, None, None]
    n = idx.shape[-1]
    ksel = ks_blk[bi, gi, idx].reshape(B, C_KV_HEADS, Tq, n * SLC_BLK, C_DH)
    vsel = vs_blk[bi, gi, idx].reshape(B, C_KV_HEADS, Tq, n * SLC_BLK, C_DH)
    qg = q.reshape(B, Tq, C_KV_HEADS, C_GROUP, C_DH)
    s = jnp.einsum('btghd,bgtjd->bghtj', qg, ksel) * ATT_SCALE
    kpos = (idx[..., None] * SLC_BLK + jnp.arange(SLC_BLK)).reshape(B, C_KV_HEADS, Tq, n * SLC_BLK)
    mask = (kpos <= pos[None, None, :, None])[:, :, None]
    p = masked_softmax(s, mask)
    o = jnp.einsum('bghtj,bgtjd->btghd', p.astype(vsel.dtype), vsel)
    return o.reshape(B, Tq, C_HEADS, C_DH)

def slc_attention_blocked(q, pos, idx, ks_blk, vs_blk):
    B, T = q.shape[:2]
    nq = T // SLC_QBLK
    qc = q.reshape(B, nq, SLC_QBLK, C_HEADS, C_DH).swapaxes(0, 1)
    pc = pos.reshape(nq, SLC_QBLK)
    ic = idx.reshape(B, C_KV_HEADS, nq, SLC_QBLK, -1).transpose(2, 0, 1, 3, 4)
    oc = lax.map(lambda a: slc_attention(a[0], a[1], a[2], ks_blk, vs_blk), (qc, pc, ic))
    return oc.swapaxes(0, 1).reshape(B, T, C_HEADS, C_DH)

def win_attention_banded(q, kw, vw):
    B, T = q.shape[:2]
    nb = T // Q_BLK
    span = WINDOW + Q_BLK
    kp = jnp.pad(kw, ((0, 0), (WINDOW, 0), (0, 0), (0, 0)))
    vp = jnp.pad(vw, ((0, 0), (WINDOW, 0), (0, 0), (0, 0)))
    kidx = jnp.arange(nb)[:, None] * Q_BLK + jnp.arange(span)[None, :]
    kb, vb = kp[:, kidx], vp[:, kidx]
    kpos = (kidx - WINDOW)[:, None, :]
    qpos = jnp.arange(T).reshape(nb, Q_BLK)[:, :, None]
    mask = (kpos <= qpos) & (kpos > qpos - WINDOW) & (kpos >= 0)
    qb = q.reshape(B, nb, Q_BLK, C_KV_HEADS, C_GROUP, C_DH)
    s = jnp.einsum('bnqghd,bnkgd->bghnqk', qb, kb) * ATT_SCALE
    p = masked_softmax(s, mask)
    o = jnp.einsum('bghnqk,bnkgd->bnqghd', p.astype(vb.dtype), vb)
    return o.reshape(B, T, C_HEADS, C_DH)

def win_attention_cached(q, pos, kw, vw, kpos):
    B, Tq = q.shape[:2]
    qg = q.reshape(B, Tq, C_KV_HEADS, C_GROUP, C_DH)
    s = jnp.einsum('btghd,bkgd->bghtk', qg, kw) * ATT_SCALE
    mask = (kpos[None, :] <= pos[:, None]) & (kpos[None, :] > pos[:, None] - WINDOW)
    p = masked_softmax(s, mask)
    o = jnp.einsum('bghtk,bkgd->btghd', p.astype(vw.dtype), vw)
    return o.reshape(B, Tq, C_HEADS, C_DH)

def trunk_layer(x, c, pos, w, past_kv, win_buf, s0, h0, conv0, is_prompt):
    (ada_w, ada_b, w_in, lb, a_norm_g, conv_w, conv_b, ga_w, ga_b, gx_w, gx_b, lam,
     cmp_pos, cmp_w1, cmp_w2, w_branch, w_out, ln_g, ln_b) = w
    B, T, D = x.shape
    shift, scale, gate = jnp.split(c @ ada_w + ada_b, 3, axis=-1)
    h = x * (1.0 + scale[:, None]) + shift[:, None]
    splits = np.cumsum(IN_SIZES)[:-1].tolist()
    aq, af, ai, az, bx, bz, cq, ckv, cg, cz, mg = jnp.split(h @ w_in, splits, axis=-1)

    qa = jax.nn.silu(aq).reshape(B, T, A_HEADS, A_DK)
    log_f = jnp.logaddexp(jnp.log(lb), jnp.log1p(-lb) + jax.nn.log_sigmoid(af.astype(jnp.float32)))
    ka = -jnp.expm1(log_f)
    hg = (qa, ka.reshape(B, T, A_HEADS, A_DK), ai.reshape(B, T, A_HEADS, A_DV), log_f.reshape(B, T, A_HEADS, A_DK))
    if is_prompt:
        oa, s_new = hgrn2_chunked(hg[0], hg[1], hg[2], hg[3], s0)
    else:
        oa, s_new = hgrn2_recurrent(hg[0], hg[1], hg[2], hg[3], s0)
    ya = (group_rms(oa).reshape(B, T, A_WIDTH) * a_norm_g).astype(x.dtype) * jax.nn.silu(az)

    yb, h_new, conv_new = rglru_branch(bx, bz, conv0, h0, conv_w, conv_b, ga_w, ga_b, gx_w, gx_b, lam)

    q = cq.reshape(B, T, C_HEADS, C_DH)
    q_rot = rope(q, pos)
    kv = ckv.reshape(B, T, 6, C_KV_HEADS, C_DH)
    new_rows = jnp.stack([kv[:, :, 0], kv[:, :, 1], rope(kv[:, :, 2], pos), kv[:, :, 3]], axis=2)
    win_rows = jnp.stack([rope(kv[:, :, 4], pos), kv[:, :, 5]], axis=2)
    if is_prompt:
        full = new_rows
    else:
        full = jnp.concatenate([past_kv.astype(new_rows.dtype), new_rows], axis=1)
    L = full.shape[1]
    kc, vc = compress(full[:, :, 0:2], cmp_pos, cmp_w1, cmp_w2)
    o_cmp, p_cmp = cmp_attention(q, pos, kc, vc)
    n_slc = -(-L // SLC_BLK)
    idx = select_blocks(p_cmp, pos, n_slc)
    ks_blk = to_blocks(full[:, :, 2], n_slc)
    vs_blk = to_blocks(full[:, :, 3], n_slc)
    if is_prompt:
        o_slc = slc_attention_blocked(q_rot, pos, idx, ks_blk, vs_blk)
        o_win = win_attention_banded(q_rot, win_rows[:, :, 0], win_rows[:, :, 1])
        win_new = win_rows[:, T - min(WINDOW, T):]
    else:
        o_slc = slc_attention(q_rot, pos, idx, ks_blk, vs_blk)
        wb = win_buf.shape[1]
        wkv = jnp.concatenate([win_buf.astype(win_rows.dtype), win_rows], axis=1)
        wpos = pos[0] - wb + jnp.arange(wb + T)
        o_win = win_attention_cached(q_rot, pos, wkv[:, :, 0], wkv[:, :, 1], wpos)
        win_new = wkv[:, T:]
    g3 = jax.nn.sigmoid(cg).reshape(B, T, 3, C_HEADS, 1)
    oc = g3[:, :, 0] * o_cmp + g3[:, :, 1] * o_slc + g3[:, :, 2] * o_win
    yc = oc.reshape(B, T, C_WIDTH).astype(x.dtype) * jax.nn.silu(cz)

    ys = jnp.stack([ya, yb, yc], axis=2)
    branch = jnp.einsum('btnc,ncd->btnd', ys, w_branch)
    merged = jnp.sum(jax.nn.sigmoid(mg).reshape(B, T, N_BRANCH, D) * branch, axis=2)
    out = merged @ w_out
    x_new = layer_norm(ALPHA * x + gate[:, None] * out, ln_g, ln_b)
    return x_new, (new_rows, win_new, s_new, h_new, conv_new)

def setup_inputs(seed: int = 0) -> dict:
    key = jax.random.key(seed)
    ks = jax.random.split(key, 30)
    f32 = jnp.float32

    def nrm(k, shape, s):
        return jax.random.normal(k, shape, f32) * s

    n_pages = PAST_LEN // PAGE_SIZE
    n_pool = (5 * DEC_BATCH * n_pages) // 4
    win_buf = min(WINDOW, PAST_LEN)
    page_table = jax.random.permutation(ks[5], n_pool)[:DEC_BATCH * n_pages].reshape(DEC_BATCH, n_pages).astype(jnp.int32)
    a_init = jax.random.uniform(ks[21], (DEPTH, B_WIDTH), f32, 0.9, 0.999)
    return {
        'x_prompt': nrm(ks[0], (BATCH, SEQ, D_MODEL), 1.0),
        'x_sample': nrm(ks[1], (DEC_BATCH, DEC_SEQ, D_MODEL), 1.0),
        'c_prompt': nrm(ks[2], (BATCH, D_MODEL), 1.0),
        'c_sample': nrm(ks[3], (DEC_BATCH, D_MODEL), 1.0),
        'cache_nsa_kv': nrm(ks[4], (DEPTH, n_pool, PAGE_SIZE, 4, C_KV_HEADS, C_DH), 1.0),
        'page_table': page_table,
        'state_win_kv': nrm(ks[6], (DEPTH, DEC_BATCH, win_buf, 2, C_KV_HEADS, C_DH), 1.0),
        'state_hgrn': nrm(ks[7], (DEPTH, DEC_BATCH, A_HEADS, A_DK, A_DV), 0.3),
        'state_rglru': nrm(ks[8], (DEPTH, DEC_BATCH, B_WIDTH), 0.5),
        'state_conv': nrm(ks[9], (DEPTH, DEC_BATCH, CONV_W - 1, B_WIDTH), 1.0),
        'ada_w': nrm(ks[10], (DEPTH, D_MODEL, 3 * D_MODEL), 0.5 * D_MODEL ** -0.5),
        'ada_b': nrm(ks[11], (DEPTH, 3 * D_MODEL), 0.02),
        'w_in': nrm(ks[12], (DEPTH, D_MODEL, N_IN), D_MODEL ** -0.5),
        'a_lb': nrm(ks[13], (DEPTH, A_WIDTH), 1.0),
        'a_norm_g': 1.0 + nrm(ks[14], (DEPTH, A_WIDTH), 0.02),
        'b_conv_w': nrm(ks[15], (DEPTH, CONV_W, B_WIDTH), CONV_W ** -0.5),
        'b_conv_b': nrm(ks[16], (DEPTH, B_WIDTH), 0.02),
        'b_gate_a_w': nrm(ks[17], (DEPTH, B_BLOCKS, B_BW, B_BW), B_BW ** -0.5),
        'b_gate_a_b': nrm(ks[18], (DEPTH, B_WIDTH), 0.02),
        'b_gate_x_w': nrm(ks[19], (DEPTH, B_BLOCKS, B_BW, B_BW), B_BW ** -0.5),
        'b_gate_x_b': nrm(ks[20], (DEPTH, B_WIDTH), 0.02),
        'b_lambda': jnp.log(a_init) - jnp.log1p(-a_init),
        'c_cmp_pos': nrm(ks[22], (DEPTH, 2, CMP_LEN, C_DH), 0.02),
        'c_cmp_w1': nrm(ks[23], (DEPTH, 2, CMP_LEN * C_DH, C_DH), (CMP_LEN * C_DH) ** -0.5),
        'c_cmp_w2': nrm(ks[24], (DEPTH, 2, C_DH, C_DH), C_DH ** -0.5),
        'w_branch': nrm(ks[25], (DEPTH, N_BRANCH, BR_WIDTH, D_MODEL), BETA * BR_WIDTH ** -0.5),
        'w_out': nrm(ks[26], (DEPTH, D_MODEL, D_MODEL), BETA * D_MODEL ** -0.5),
        'ln_g': 1.0 + nrm(ks[27], (DEPTH, D_MODEL), 0.02),
        'ln_b': nrm(ks[28], (DEPTH, D_MODEL), 0.02),
    }

def reference(x_prompt, x_sample, c_prompt, c_sample, cache_nsa_kv, page_table, state_win_kv, state_hgrn,
              state_rglru, state_conv, ada_w, ada_b, w_in, a_lb, a_norm_g, b_conv_w, b_conv_b, b_gate_a_w,
              b_gate_a_b, b_gate_x_w, b_gate_x_b, b_lambda, c_cmp_pos, c_cmp_w1, c_cmp_w2, w_branch, w_out,
              ln_g, ln_b):
    lb_all = jnp.cumsum(jax.nn.softmax(a_lb.astype(jnp.float32), axis=0), axis=0)
    lb_all = lb_all - lb_all[0:1]
    n_pages = page_table.shape[1]
    past_len = n_pages * cache_nsa_kv.shape[2]
    bp, seq = x_prompt.shape[:2]
    bs, ts = x_sample.shape[:2]
    pos_p = jnp.arange(seq)
    pos_s = past_len + jnp.arange(ts)
    xp, xs = x_prompt, x_sample
    st_prompt, st_sample = [], []
    for l in range(DEPTH):
        w = (ada_w[l], ada_b[l], w_in[l], lb_all[l], a_norm_g[l], b_conv_w[l], b_conv_b[l],
             b_gate_a_w[l], b_gate_a_b[l], b_gate_x_w[l], b_gate_x_b[l], b_lambda[l],
             c_cmp_pos[l], c_cmp_w1[l], c_cmp_w2[l], w_branch[l], w_out[l], ln_g[l], ln_b[l])
        xp, sp = trunk_layer(xp, c_prompt, pos_p, w, None, None,
                             jnp.zeros((bp, A_HEADS, A_DK, A_DV), xp.dtype),
                             jnp.zeros((bp, B_WIDTH), xp.dtype),
                             jnp.zeros((bp, CONV_W - 1, B_WIDTH), xp.dtype), True)
        past = cache_nsa_kv[l][page_table].reshape(bs, past_len, 4, C_KV_HEADS, C_DH)
        xs, ss = trunk_layer(xs, c_sample, pos_s, w, past, state_win_kv[l], state_hgrn[l],
                             state_rglru[l], state_conv[l], False)
        st_prompt.append(sp)
        st_sample.append(ss)
    nsa_p = jnp.stack([s[0] for s in st_prompt], axis=0)
    nsa_s = jnp.stack([s[0] for s in st_sample], axis=0)
    win_p = jnp.stack([s[1] for s in st_prompt], axis=0)
    win_s = jnp.stack([s[1] for s in st_sample], axis=0)
    hg_p = jnp.stack([s[2] for s in st_prompt], axis=0)
    hg_s = jnp.stack([s[2] for s in st_sample], axis=0)
    rg_p = jnp.stack([s[3] for s in st_prompt], axis=0)
    rg_s = jnp.stack([s[3] for s in st_sample], axis=0)
    cv_p = jnp.stack([s[4] for s in st_prompt], axis=0)
    cv_s = jnp.stack([s[4] for s in st_sample], axis=0)
    return (xp, xs, nsa_p, nsa_s, win_p, win_s, hg_p, hg_s, rg_p, rg_s, cv_p, cv_s)


_drawn_inputs = setup_inputs


def setup_inputs(seed=0):
    import zlib

    import numpy as np

    out = dict(_drawn_inputs(seed))
    spreads = {}
    factors = {'cache_nsa_kv': 8.0,
     'a_norm_g': 8.0,
     'b_gate_a_b': 8.0,
     'b_gate_x_b': 8.0,
     'c_cmp_pos': 8.0,
     'c_cmp_w1': 4.085,
     'c_cmp_w2': 2.752,
     'ln_g': 3.112,
     'ln_b': 2.739}
    for name, (base, spread) in spreads.items():
        noise = np.random.default_rng([zlib.crc32(name.encode()), seed]).standard_normal(out[name].shape)
        drawn = base * np.exp(spread * noise) if base else spread * noise
        out[name] = __import__('jax').numpy.asarray(drawn.astype(out[name].dtype))
    for name, factor in factors.items():
        out[name] = (out[name] * factor).astype(out[name].dtype)
    return out
```

```python
import concourse.bass as bass
from concourse import mybir

F32 = mybir.dt.float32
F32R = mybir.dt.float32r
BF16 = mybir.dt.bfloat16
I32 = mybir.dt.int32
ALU = mybir.AluOpType
ACT = mybir.ActivationFunctionType
AX = mybir.AxisListType.X
MUL, ADD, SUB, MAX, MIN = ALU.mult, ALU.add, ALU.subtract, ALU.max, ALU.min

P = 128
D = 1024
KT = D // P
NS = 8
T = 1024
NT = T // P
TC = NS + T
CH = TC // 3
W = 512
HD = 64
NCMP = 63
C0 = 4 * W + 2 * W
CKV = C0 + W
CCG = CKV + 768
CCZ = CCG + 24
CMG = CCZ + W
ALPHA = 2.0 ** 0.25
EPS = 1e-5
SCALE = HD ** -0.5
NEG = -1e30
LRU_C = 8.0
LEVELS = [64, 32, 16, 8, 4, 2, 1]
XR = 128 * 2

BASE = 16512
END = (229368 - BASE) // 4
O_H = 0
O_G = O_H + 2 * KT * TC
O_CS = O_G + 1272
O_RAW = O_CS + 2328
O_W = O_RAW + 3 * 1024
O_F = O_W + 8192


def constants():
    import numpy as np
    g = np.zeros((P, GN), np.float32)
    g[:, 0:128] = np.eye(P)
    r = np.arange(P)
    for b in range(NS):
        g[b, GE8 + 8 * b:GE8 + 8 * b + 8] = 1
        g[8 * b:8 * b + 8, GE64 + b] = 1
    for p in range(64):
        g[p, GHM + p % 8] = 1
        g[p, GGM + (p % 8) // 4] = 1
    for p in range(8):
        g[p, GG8 + 4 * (p // 4):GG8 + 4 * (p // 4) + 4] = 1
    g[:, GRV] = r >= 31
    g[:, GEPS] = EPS
    g[:, GIO:GIO + 16] = np.arange(16)
    inv = 10000.0 ** (-np.arange(0, HD, 2, dtype=np.float32) / np.float32(HD))
    inv = inv.astype(np.float32)

    def rope(pos):
        ang = (pos.astype(np.float32)[:, None] * inv[None, :]).astype(np.float32)
        c, s = np.cos(ang), np.sin(ang)
        return np.concatenate([c, c, s, -s], 1).astype(np.float32)
    g[:, GRP:GRP + 128] = rope(np.full(P, T))
    c = np.zeros((P, 1792), np.float32)
    for t in range(NT):
        c[:, 128 * t:128 * t + 128] = rope(r + P * t)
        end = np.arange(64) * 16 + 31
        ok = (end[None, :] <= (P * t + r)[:, None]) & (np.arange(64) < NCMP)[None, :]
        c[:, 1024 + 64 * t:1024 + 64 * t + 64] = np.where(ok, 0, NEG)
    c[:, 1536:1664] = np.where(r[None, :] <= r[:, None], 0, NEG)
    c[:, 1664:1792] = np.where(r[None, :] > r[:, None], 0, NEG)
    a = np.zeros((P, 2176), np.float32)
    s, t = r[:, None], r[None, :]
    for i, m in enumerate(LEVELS):
        a[:, 128 * i:128 * i + 128] = (s // (2 * m) == t // (2 * m)) & (s // m % 2 == 0) & (t // m % 2 == 1)
    a[:, 896:1024] = s == t
    a[:, 1024:2048] = np.arange(1024)[None, :] % P != 0
    a[:, 2048:2176] = 1
    return g, c, a


GE8, GE64, GHM, GGM, GG8, GRV, GEPS, GIO, GRP, GN = 128, 192, 200, 208, 210, 218, 219, 220, 236, 368


class Ring:

    def __init__(self, nc, ctx, name, slots):
        self.full = ctx.enter_context(nc.semaphore(name + "_full"))
        self.free = ctx.enter_context(nc.semaphore(name + "_free"))
        self.p, self.c = 0, 0
        self.p0, self.c0 = 0, 0
        self.pslots = self.cslots = slots

    def restart_filling(self, slots):
        self.p0, self.pslots = self.p, slots

    def restart_emptying(self, slots):
        self.c0, self.cslots = self.c, slots

    def acquire(self, eng):
        if self.p - self.p0 >= self.pslots:
            eng.wait_ge(self.free, self.p - self.pslots + 1)
        self.p += 1
        return (self.p - self.p0 - 1) % self.pslots

    def take(self, eng):
        self.c += 1
        eng.wait_ge(self.full, self.c)
        return (self.c - self.c0 - 1) % self.cslots


class Steps:

    def __init__(self, eng, own):
        self.eng, self.own, self.n = eng, own, {}

    def fire(self, ins, sem):
        ins.then_inc(sem, 1)
        self.n[sem.name] = self.n.get(sem.name, 0) + 1
        return self.n[sem.name]

    def mark(self, sem):
        self.eng.sem_inc(sem, 1)
        self.n[sem.name] = self.n.get(sem.name, 0) + 1

    def __call__(self, ins, sem=None):
        sem = sem or self.own
        self.eng.wait_ge(sem, self.fire(ins, sem))


def w_units():
    u = [("cq0", [(C0, 256)], 2), ("cq1", [(C0 + 256, 256)], 2), ("cmp", [(CKV, 256)], 2),
         ("slc", [(CKV + 256, 256)], 2), ("win", [(CKV + 512, 256)], 2), ("cg", [(CCG, 24)], 2),
         ("cz0", [(CCZ, 256)], 2), ("cz1", [(CCZ + 256, 256)], 2)]
    for h in range(4):
        u.append(("aqf", [(P * h, P), (W + P * h, P)], 2))
        u.append(("aiz", [(2 * W + P * h, P), (3 * W + P * h, P)], 2))
    for j in range(4):
        u.append(("bxz", [(4 * W + P * j, P), (5 * W + P * j, P)], 2))
    for n in (1, 0, 2):
        for dp in range(4):
            u.append(("mg", [(CMG + n * D + 256 * dp, 256)], 2))
            u.append(("br%d" % n, [(256 * dp, 256)], 1))
    for q in range(4):
        u.append(("out", [(256 * q, 256)], 2))
    return u


UNITS = w_units()
U_CZ, U_A, U_B, U_M, U_O = 6, 8, 16, 20, 44


def attention_units():
    u = []
    for t in range(NT):
        u.append((0, t, 0, 0, 0, 4))
        for k in (1, 2):
            for hh in range(4):
                for g in range(2):
                    n = t + 1 if k == 1 else min(t + 1, 5)
                    u.append((k, t, hh, g, t + 1 - n, n))
    return u


AU = attention_units()


def layer_program(nc, ctx, a, o):
    def sb(name, off, shape, dt=F32, parts=P):
        n = 1
        for x in shape:
            n *= x
        size = n * (2 if dt == BF16 else 4)
        assert 4 * off + size <= 4 * END, (name, off, size)
        t = nc.alloc_sbuf_tensor_at(name, [parts] + list(shape), dt, offset=BASE + 4 * off)
        return t[tuple([slice(None)] * (len(shape) + 1))]

    def sem(name):
        return ctx.enter_context(nc.semaphore(name))

    ps = ctx.enter_context(nc.psum_tensor("ps", [P, 8, 512], F32))
    H = [sb("h_hi", O_H, [KT, TC], F32R), sb("h_lo", O_H + KT * TC, [KT, TC], F32R)]
    Hf = [x.bitcast(F32) for x in H]
    G = sb("const_g", O_G, [GN])
    ID = G[:, 0:128]
    o_ = O_G + GN
    MOD = sb("mod", o_, [24, 9]); o_ += 216
    PRM = sb("prm", o_, [60]); o_ += 64
    CST = sb("cst", o_, [4, 32]); o_ += 128
    G3 = sb("g3", o_, [NT, 24]); o_ += 192
    SM = sb("sm", o_, [2, 24]); o_ += 48
    NM = sb("nm", o_, [8]); o_ += 8
    CW = sb("cw", o_, [24]); o_ += 24
    PB = sb("posbias", o_, [2]); o_ += 8
    C8 = sb("c8", o_, [8]); o_ += 8
    LN = sb("ln", o_, [32]); o_ += 32
    KP = sb("pages", o_, [64], I32); o_ += 64
    assert o_ <= O_CS, o_
    CS = sb("cs", O_CS, [1816], parts=NS)
    CSR = sb("csr", O_CS + 1816, [512], parts=NS)
    RAW = sb("w_raw", O_RAW, [3, 4, 256])
    WS = [[sb("w%d_%s" % (i, x), O_W + 4096 * i + 2048 * j, [8, 256], F32R) for j, x in enumerate(("hi", "lo"))]
          for i in range(2)]
    WX = [[sb("w%d_%s" % (i, x), O_F + 12384 + 4096 * (i - 2) + 2048 * j, [8, 256], F32R)
           for j, x in enumerate(("hi", "lo"))] for i in (2, 3)]

    def wslot(u):
        if u < U_O:
            return WS[u % 2]
        return (WS + WX)[u - U_O]

    XIN = sb("xin", O_F, [NT, D])
    ADW = sb("adw", O_F + 8192, [4, 8, 256])
    HRAW = sb("hraw", O_F + 16384, [2, T])
    o_ = O_F + 18432
    XS = sb("xs", o_, [D], parts=NS)
    C9 = sb("c9", o_ + 1024, [D], parts=9)
    PRMR = sb("prmr", o_ + 2048, [P], parts=60)
    CSTR = sb("cstr", o_ + 2176, [W], parts=32)
    CT = sb("ct", o_ + 2688, [8, 9])
    HRS = sb("hrs", o_ + 2760, [8, 8])
    KV = sb("kv", O_F, [NT, 768])
    KTT = sb("kt", O_F + 6144, [4, T])
    QRT = sb("qrt", O_F + 10240, [4, T])
    CC = sb("const_c", O_F + 14336, [1792])
    QT = sb("qt", O_F + 16128, [4, T])
    o_ = O_F + 20224
    QTOK = sb("qtok", o_, [512])
    QRTOK = sb("qrtok", o_ + 512, [512])
    RTA = sb("rta", o_ + 1024, [256])
    RTB = sb("rtb", o_ + 1280, [256])
    HKV = sb("hkv", o_, [2, P])
    KCB = sb("kcb", o_ + 256, [P])
    VCB = sb("vcb", o_ + 384, [P])
    W2B = sb("w2b", o_ + 512, [2, P])
    POSR = sb("posr", o_ + 768, [2, HD], parts=64)
    POST = sb("post", o_ + 896, [64])
    W1B = sb("w1b", O_W, [2, 32, P])
    PR = sb("pr", O_W, [3, 1024])
    PT = sb("pt", O_W + 3072, [2, 1024])
    SC = sb("sc", O_W + 5120, [512])
    TO = sb("to", O_W + 5632, [2, 512])
    W1S = sb("w1s", O_W + 6144, [2, 16, HD])
    o_ = O_F
    PG = sb("pg", o_, [2, 8, 256]); o_ += 4096
    PGC = sb("pgc", o_, [2, 4, 512]); o_ += 4096
    WR = sb("wr", o_, [2, 4, 256]); o_ += 2048
    CMT = sb("cmt", o_, [2, 2, 512]); o_ += 2048
    KST = sb("kst", o_, [T]); o_ += 1024
    KWT = sb("kwt", o_, [512]); o_ += 512
    SRW = sb("srw", o_, [1040], parts=8); o_ += 1040
    assert o_ <= O_F + 16128
    o_ = O_F + 20224
    W2S = sb("w2s", o_, [2, HD], parts=64); o_ += 128
    HKS = sb("hks", o_, [2, 2 * NCMP], parts=64); o_ += 256
    KCS = sb("kcs", o_, [64]); o_ += 64
    VCS = sb("vcs", o_, [P], parts=64); o_ += 128
    PCS = sb("pcs", o_, [72], parts=8); o_ += 72
    SEL = sb("sel", o_, [112], parts=8); o_ += 112
    QBD = sb("qbd", o_, [2, 64]); o_ += 128
    NKT = sb("nkt", o_, [8]); o_ += 8
    PTS = sb("pts", o_, [112]); o_ += 112
    OTS = sb("ots", o_, [3, 64]); o_ += 192
    SM8 = sb("sm8", o_, [16], parts=8); o_ += 16
    assert o_ <= END
    o_ = O_F + 14864
    PW8 = sb("pw8", o_, [512], parts=8); o_ += 512
    NVR = sb("nvr", o_, [2, P], parts=1); o_ += 256
    assert o_ <= O_F + 16128
    EXQ = sb("exq", O_F, [512], parts=64)
    QROW = sb("qrow", O_F + 512, [2, P], parts=64)
    YF = sb("yf", O_F, [4, TC])
    SGZ = sb("sgz", O_F + 4128, [2, 512])
    YTK = sb("ytk", O_F + 5152, [2, 512])
    o_ = O_F + 6176
    CGX = sb("cgx", o_, [24], parts=64)
    GX = sb("gx", o_ + 24, [3], parts=64)
    CZX = sb("czx", o_ + 32, [512], parts=64)
    CZ1 = sb("cz1", o_ + 544, [64], parts=64)
    CZ2 = sb("cz2", o_ + 608, [64], parts=64)
    OSB = sb("osb", o_ + 672, [3, 64], parts=64)
    YSM = sb("ysm", o_ + 864, [512], parts=64)
    o_ = O_F
    LM = sb("lm", o_, [8, P], BF16); o_ += 512
    RM = sb("rm", o_, [T], BF16); o_ += 512
    ONES = sb("ones", o_, [P]); o_ += 128
    AS = []
    for i in range(2):
        AS.append(dict(q=sb("aq%d" % i, o_, [TC]), k=sb("ak%d" % i, o_ + TC, [TC]),
                       b=sb("ab%d" % i, o_ + 2 * TC, [TC]), z=sb("az%d" % i, o_ + 3 * TC, [TC]),
                       v=sb("av%d" % i, o_ + 4 * TC, [NT, P]), vs=sb("avs%d" % i, o_ + 4 * TC + T, [P], parts=NS)))
        o_ += 4 * TC + T + 128
    XQ = sb("xq", o_, [2, 9, XR]); o_ += 2 * 9 * XR
    DD = sb("dd", o_, [2, XR]); o_ += 2 * XR
    EL = sb("el", o_, [2, 2]); o_ += 8
    SGA = sb("sga", o_, [TC]); o_ += TC
    MSK = sb("msk", o_, [8, P]); o_ += 1024
    STA = sb("sta", o_, [P]); o_ += 128
    KOT = sb("kot", o_, [2, P]); o_ += 256
    YA = sb("ya", o_, [TC]); o_ += TC
    assert o_ <= END, o_ - END
    CA = sb("const_a", O_F + 1152 + 5280, [2176])
    STS = sb("sts", O_CS, [NS, P])
    OT = sb("ot", O_CS + 1024, [TC])
    ATT = sb("att", O_CS + 2056, [2, P])
    YH = [sb("y_hi", O_F, [4, TC], F32R), sb("y_lo", O_F + 4 * TC, [4, TC], F32R)]
    o_ = O_F + 8 * TC
    BXP = sb("bxp", o_, [2, 8 + 3 + T]); o_ += 2 * 1040
    BZ = sb("bz", o_, [2, TC]); o_ += 2 * TC
    BU = sb("bu", o_, [2, TC]); o_ += 2 * TC
    BR = sb("br", o_, [TC]); o_ += TC
    BI = sb("bi", o_, [TC]); o_ += TC
    BA = sb("ba", o_, [TC]); o_ += TC
    BT = sb("bt", o_, [TC]); o_ += TC
    BHS = sb("bhs", o_, [TC]); o_ += TC
    GWB = sb("gwb", o_, [2, 2, P]); o_ += 512
    OCO = sb("oco", o_, [2, 32]); o_ += 64
    OCR = sb("ocr", o_, [4, P], parts=32); o_ += 512
    assert o_ <= END, o_ - END
    ACC = sb("acc", O_F + 8 * TC, [8, TC])
    o_ = O_F + 16 * TC
    SGM = sb("sgm", o_, [2, TC]); o_ += 2 * TC
    TMM = sb("tmm", o_, [CH]); o_ += CH
    YST = sb("yst", o_, [TC * 2]); o_ += 2 * TC
    assert o_ <= END, o_ - END
    GB = sb("gb", O_CS, [D])
    GSR = sb("gsr", O_CS + 1024, [D], parts=9)
    XRL = sb("xrl", O_F, [3, D])
    RR = sb("rr", O_F + 3072, [2, D])
    YY = sb("yy", O_F + 5120, [2, D])
    LNG = sb("lng", O_F + 7168, [D])
    LNB = sb("lnb", O_F + 8192, [D])
    BST = sb("bst", O_F + 9216, [2, 6])
    BAG = sb("bag", O_F + 9232, [4])

    scratch = [nc.dram_tensor("y_spill%d" % n, [P, 4, TC], F32, kind="Internal").ap() for n in range(2)]
    win = a["w_in"][0]
    const_g, const_c, const_a = a["const_g"], a["const_c"], a["const_a"]

    ld = {n: sem("ld_" + n) for n in ("g", "x", "cc", "w1", "lng", "sts", "yst")}
    adw_in = [sem("adw_in%d" % i) for i in range(4)]
    raw_in = [sem("raw_in%d" % i) for i in range(3)]
    gw_in = [sem("gw_in%d" % i) for i in range(2)]
    pg_in = [sem("pg_in%d" % i) for i in range(2)]
    pgc_in = [sem("pgc_in%d" % i) for i in range(2)]
    outs = sem("outs")
    spilled = sem("spilled")
    half_split = sem("half_split")
    w_used = sem("w_used")
    own = {n: sem("own_" + n) for n in ("act", "dve", "pool")}
    R = {}

    def ring(name, slots):
        R[name] = Ring(nc, ctx, name, slots)
        return R[name]

    ev = {}

    def e(name):
        if name not in ev:
            ev[name] = sem(name)
        return ev[name]

    halves_before = [0]
    for u in UNITS:
        halves_before.append(halves_before[-1] + u[2])
    NHALF = halves_before[-1]

    act3 = ring("xt", 6)
    hraw_ring = ring("hraw", 2)
    p1 = ring("p1", 4)
    tq = ring("tq", 2)
    tr = ring("tr", 2)
    ta = ring("ta", 1)
    tv = ring("tv", 1)
    sa = ring("sa", 2)
    sv = ring("sv", 1)
    pz = ring("pz", 4)
    tz = ring("tz", 2)
    pq = ring("pq", 2)
    pf = ring("pf", 2)
    y_sent = [sem("y_sent%d" % i) for i in range(2)]
    yp = o["y_prompt"][0].rearrange("(t p) d -> p t d", p=P)

    def y_out(sp, t):
        sp.wait_ge(e("y_ready"), t + 1)
        if t:
            sp.dma_start(yp[:, t - 1], YY[:, t % 2]).then_inc(y_sent[t % 2], 16)
        else:
            sp.dma_start(o["y_sample"].rearrange("b t d -> (b t) d"), YY[0:8, 0]).then_inc(y_sent[0], 16)

    def yc_transposes(pe, t):
        pe.wait_ge(e("yc_tok"), t)
        b = tz.acquire(pe)
        for i in range(4):
            last = nc.tensor.transpose(ps[:, 4 + b, P * i:P * i + P], YTK[:, (t - 1) % 2, P * i:P * i + P], ID)
        last.then_inc(tz.full, 1)

    def yc_out(act, st, t):
        q = tz.take(act)
        st(nc.scalar.activation(YF[:, :, NS + P * (t - 1):NS + P * t], ps[:, 4 + q, :].rearrange("p (c t) -> p c t", c=4), ACT.Copy), tz.free)

    def a_items(h):
        plan = "F P0 P1 R0 P2 R1 P3 P4 R2 P5 R3 P6 S P7 R4 P8 R5 P9 P10 R6 P11 R7 N".split()
        return [(x[0], int(x[1:] or 0)) for x in plan if (x[0] == "P" and h < 4) or (x[0] != "P" and h > 0)]

    block = ctx.enter_context(nc.Block())

    @block.sync
    def _(sp):
        total = [0]

        def out_dma(dst, src):
            sp.dma_start(dst, src).then_inc(outs, 16)
            total[0] += 16

        for k, src in ((0, a["c_sample"]), (8, a["c_prompt"])):
            sp.dma_start(C9[k:k + src.shape[0], :], src).then_inc(ld["g"], 16)
        sp.dma_start(G, const_g).then_inc(ld["g"], 16)
        r = 0
        for n in ("ada_b", "a_norm_g", "b_conv_w", "b_conv_b", "b_gate_a_b", "b_gate_x_b", "b_lambda"):
            src = a[n]
            src = (src[0] if len(src.shape) == 2 else src[0].rearrange("w c -> (w c)")).rearrange("(j p) -> j p", p=P)
            sp.dma_start(PRMR[r:r + src.shape[0], :], src).then_inc(ld["g"], 16)
            r += src.shape[0]
        sp.dma_start(CSTR[0:24, :], a["state_conv"][0].rearrange("b w c -> (b w) c")).then_inc(ld["g"], 16)
        sp.dma_start(CSTR[24:32, :], a["state_rglru"][0]).then_inc(ld["g"], 16)
        sp.dma_start(XS, a["x_sample"].rearrange("b t d -> (b t) d")).then_inc(ld["x"], 16)
        adv = a["ada_w"][0].rearrange("(k p) n -> p k n", p=P)
        xv = a["x_prompt"][0].rearrange("(t p) d -> p t d", p=P)
        for i in range(12):
            if i >= 4:
                sp.wait_ge(e("ada_used"), i - 3)
            sp.dma_start(ADW[:, i % 4], adv[:, :, 256 * i:256 * i + 256]).then_inc(adw_in[i % 4], 16)
            if i < 8:
                sp.dma_start(XIN[:, i], xv[:, i]).then_inc(ld["x"], 16)

        half = [0]

        def load_half(u, hf):
            name, runs, nh = UNITS[u]
            n = half[0]
            half[0] += 1
            if n >= 3:
                sp.wait_ge(half_split, n - 2)
            c = 0
            for col, w in runs:
                if name.startswith("br"):
                    src = a["w_branch"][0, int(name[2])].rearrange("(k p) n -> p k n", p=P)[:, :, col:col + w]
                elif name == "out":
                    src = a["w_out"][0].rearrange("(k p) n -> p k n", p=P)[:, 4 * hf:4 * hf + 4, col:col + w]
                else:
                    src = win.rearrange("(k p) n -> p k n", p=P)[:, 4 * hf:4 * hf + 4, col:col + w]
                sp.dma_start(RAW[:, n % 3, :, c:c + w], src).then_inc(raw_in[n % 3], 16)
                c += w

        def load_unit(u):
            for hf in range(UNITS[u][2]):
                load_half(u, hf)

        load_unit(0)
        sp.wait_ge(e("h_ready"), 1)
        sp.dma_start(CC, const_c).then_inc(ld["cc"], 16)
        for u in range(1, 6):
            load_unit(u)
        sp.wait_ge(e("cs_roped"), 1)
        nsa_s = o["nsa_kv_sample"].rearrange("l b t f g d -> (l b t) (f g d)")
        win_s = o["win_kv_sample"][0].rearrange("b w f g d -> b w (f g d)")
        out_dma(nsa_s, CS[:, 512:1024])
        out_dma(win_s[:, 511, :], CS[:, 1024:1280])
        swin = a["state_win_kv"][0].rearrange("b w f g d -> b w (f g d)")
        def load_w1(dst):
            for h in range(2):
                hp = slice(64 * h, 64 * h + 64)
                for c in range(2):
                    sp.dma_start(dst[hp, c, :, hp], a["c_cmp_w1"][0, c].rearrange("(j d) o -> d j o", d=HD)).then_inc(ld["w1"], 16)

        def load_w2(dst):
            for h in range(2):
                hp = slice(64 * h, 64 * h + 64)
                for c in range(2):
                    sp.dma_start(dst[hp, c, hp], a["c_cmp_w2"][0, c]).then_inc(ld["w1"], 16)

        sp.wait_ge(e("w1_zero"), 1)
        load_w1(W1B)
        sp.wait_ge(e("w1_zero"), 2)
        load_w2(W2B)
        for h in range(2):
            sp.dma_start(POSR[:, h, :], a["c_cmp_pos"][0].rearrange("c j d -> (c j) d")).then_inc(ld["w1"], 16)
        sp.dma_start(KP[0:1, :], a["page_table"].rearrange("b (o n) -> o (b n)", o=1)).then_inc(ld["cc"], 16)
        nsa_p = o["nsa_kv_prompt"][0, 0].rearrange("(t p) f g d -> p t (f g d)", p=P)
        win_p = o["win_kv_prompt"][0, 0].rearrange("(t p) f g d -> p t (f g d)", p=P)
        for t in range(NT):
            out_dma(nsa_p[:, t], KV[:, t, 0:512])
        out_dma(win_p, KV[:, 4:8, 512:768])
        R["kv_out"] = total[0]
        sp.wait_ge(e("s4_start"), 1)
        for c in range(2):
            sp.dma_start(W1S[:, c], a["c_cmp_w1"][0, c].rearrange("(j p) o -> p j o", p=P)).then_inc(ld["w1"], 16)
            sp.dma_start(W2S[:, c], a["c_cmp_w2"][0, c]).then_inc(ld["w1"], 16)
        sp.wait_ge(ld["cc"], 32)
        sp.wait_ge(e("q_bd"), 1)
        sp.wait_ge(outs, total[0])
        cache = a["cache_nsa_kv"][0].rearrange("n p f g d -> n p (f g d)")
        npool = cache.shape[0]
        for b in range(NS):
            def page(j):
                i = sp.value_load(KP[0:1, 8 * b + j:8 * b + j + 1], min_val=0, max_val=npool - 1)
                return cache[bass.ds(i, 1)]

            if b >= 2:
                sp.wait_ge(e("s_hid"), b - 1)
            for j in range(8):
                rows = page(j)
                hp = slice(64 * (j % 2), 64 * (j % 2) + 64)
                for par in range(2):
                    dst = PGC[hp, b % 2, j // 2, :].rearrange("q (x par d) -> q par x d", x=4, par=2)[:, par]
                    src = rows.rearrange("o (q par) c -> q par (o c)", par=2)[:, par, 0:256].rearrange("q (x d) -> q x d", x=4)
                    sp.dma_start(dst, src).then_inc(pgc_in[b % 2], 16)
            if b >= 2:
                sp.wait_ge(e("s_pv"), b - 1)
            for j in range(8):
                sp.dma_start(PG[:, b % 2, j, :], page(j).rearrange("o p c -> p (o c)")[:, 256:512]).then_inc(pg_in[b % 2], 16)
            wv = swin[b].rearrange("(t p) c -> p t c", p=P)
            sp.dma_start(WR[1:P, b % 2, 0, :], wv[1:P, 0, :]).then_inc(pg_in[b % 2], 16)
            sp.dma_start(WR[:, b % 2, 1:4, :], wv[:, 1:4, :]).then_inc(pg_in[b % 2], 16)
            sp.dma_start(WR[0:1, b % 2, 0, :], CS[b:b + 1, 1024:1280]).then_inc(pg_in[b % 2], 16)
            sp.dma_start(NVR[:, b % 2, :], CS[b:b + 1, 896:1024]).then_inc(pg_in[b % 2], 16)
        for u in range(U_CZ, U_A):
            load_unit(u)
        for b in range(NS):
            out_dma(win_s[b, 0:511, :], swin[b, 1:512, :])
        load_unit(U_A)
        load_half(U_A + 1, 0)
        sp.wait_ge(e("yc_done"), 1)
        sp.dma_start(scratch[0], YF).then_inc(spilled, 16)
        sp.dma_start(CA, const_a).then_inc(ld["cc"], 16)
        load_half(U_A + 1, 1)

        def head_out(h):
            sp.wait_ge(e("ya_done"), h + 1)
            sp.dma_start(scratch[1][:, h], YA).then_inc(spilled, 16)
            out_dma(o["hgrn_sample"][0, :, h].rearrange("b k v -> k b v"), STS)
            out_dma(o["hgrn_prompt"][0, 0, h], STA)
            sp.wait_ge(outs, total[0])
            sp.wait_ge(spilled, 16 * (h + 2))
            sp.sem_inc(e("a_free"), 1)
            if h < 3:
                sp.dma_start(STS, a["state_hgrn"][0, :, h + 1].rearrange("b k v -> k b v")).then_inc(ld["sts"], 16)

        sp.dma_start(STS, a["state_hgrn"][0, :, 0].rearrange("b k v -> k b v")).then_inc(ld["sts"], 16)
        for h in range(1, 4):
            load_unit(U_A + 2 * h)
            load_half(U_A + 2 * h + 1, 0)
            if h >= 2:
                head_out(h - 2)
            load_half(U_A + 2 * h + 1, 1)
        load_unit(U_B)
        head_out(2)
        load_unit(U_B + 1)
        head_out(3)
        for j in range(4):
            if j >= 2:
                load_unit(U_B + j)
            sp.wait_ge(e("gw_zero"), 1)
            if j >= 2:
                sp.wait_ge(e("b_done"), j - 1)
            for x, n in enumerate(("b_gate_a_w", "b_gate_x_w")):
                for q in range(2):
                    hp = slice(64 * q, 64 * q + 64)
                    sp.dma_start(GWB[hp, j % 2, x, hp], a[n][0, 2 * j + q]).then_inc(gw_in[j % 2], 16)
            if j == 0:
                out_dma(o["conv_sample"][0, :, 0:2, :], a["state_conv"][0, :, 1:3, :])
        load_unit(U_M)
        sp.wait_ge(e("oc_done"), 1)
        ocf = OCR.rearrange("p j c -> p (j c)")
        out_dma(o["conv_sample"][0, :, 2, :], ocf[0:8])
        out_dma(o["conv_prompt"][0, 0], ocf[8:11])
        out_dma(o["rglru_prompt"][0], ocf[11:12])
        out_dma(o["rglru_sample"][0], ocf[12:20])
        sp.wait_ge(outs, total[0])
        sp.sem_inc(e("b_free"), 1)
        for m in range(3):
            def y_in(hf):
                n = 2 * (m - 1) + hf
                if n:
                    sp.wait_ge(e("yst_used"), n)
                sp.dma_start(YST, scratch[2 - m][:, 2 * hf:2 * hf + 2].rearrange("p c t -> p (c t)")).then_inc(ld["yst"], 16)
            for i in range(8):
                if m and i == 0:
                    y_in(0)
                if m or i:
                    load_unit(U_M + 8 * m + i)
                if m and i == 0:
                    y_in(1)
        load_unit(U_O)
        sp.wait_ge(e("acc_split"), 1)
        for t in (LNG, a["ln_g"]), (LNB, a["ln_b"]):
            sp.dma_start(t[0], t[1][0:1].to_broadcast([P, D])).then_inc(ld["lng"], 16)
        for u in range(U_O + 1, U_O + 4):
            load_unit(u)
        for t in range(9):
            if t >= 3:
                sp.wait_ge(e("x_used"), t - 2)
            if t:
                sp.dma_start(XRL[:, t % 3], xv[:, t - 1]).then_inc(adw_in[t % 3], 16)
            else:
                sp.dma_start(XRL[0:8, 0], a["x_sample"].rearrange("b t d -> (b t) d")).then_inc(adw_in[0], 16)
            if t >= 2:
                y_out(sp, t - 2)
        for t in (7, 8):
            y_out(sp, t)
        sp.wait_ge(outs, total[0])
        for i in range(2):
            sp.wait_ge(y_sent[i], 16 * (5 - i))

    @block.gpsimd
    def _(pool):
        st = Steps(pool, own["pool"])
        n = [0]
        slot_seen = [0, 0, 0]

        def split_unit(u):
            for hf in range(UNITS[u][2]):
                split_half(u, hf)

        def split_half(u, hf):
            name, runs, nh = UNITS[u]
            width = sum(w for _, w in runs)
            hi, lo = wslot(u)
            if U_O > u >= 2:
                pool.wait_ge(w_used, u - 1)
            if u in (U_O, U_O + 1):
                pool.wait_ge(w_used, u - 1)
            if u == U_O + 2:
                pool.wait_ge(e("acc_split"), 1)
            s = n[0] % 3
            slot_seen[s] += 16 * len(runs)
            pool.wait_ge(raw_in[s], slot_seen[s])
            k = slice(4 * hf, 4 * hf + 4)
            raw = RAW[:, s, :, 0:width]
            st(nc.gpsimd.tensor_copy(hi[:, k, 0:width], raw))
            st.fire(nc.gpsimd.tensor_tensor(lo[:, k, 0:width], raw, hi[:, k, 0:width].bitcast(F32), SUB), half_split)
            n[0] += 1

        for u in range(6):
            split_unit(u)
        pool.wait_ge(w_used, 6)
        st(nc.gpsimd.memset(W1B[0:64, :, :, 64:128], 0.0))
        st(nc.gpsimd.memset(W1B[64:128, :, :, 0:64], 0.0), e("w1_zero"))
        pool.wait_ge(e("kv_done"), 1)
        st(nc.gpsimd.memset(HKV, 0.0))
        st(nc.gpsimd.memset(W2B[0:64, :, 64:128], 0.0))
        st.fire(nc.gpsimd.memset(W2B[64:128, :, 0:64], 0.0), e("w1_zero"))
        for i in range(2 * NT):
            t, k = i // 2, i % 2 + 1
            pool.wait_ge(e("o_used"), 3 * t + k + 1)
            d3 = QT[:, :, P * t:P * t + P]
            st(nc.gpsimd.tensor_tensor(d3, d3, TO[:, i % 2, :].rearrange("p (a c) -> p a c", a=4), ADD), e("to_added"))
        pool.wait_ge(e("s4_start"), 1)
        split_unit(U_CZ)
        pool.wait_ge(e("s_hid"), NS)
        for u in range(U_CZ + 1, U_A + 2):
            split_unit(u)

        def differences(h, q):
            S = AS[h % 2]
            c0 = NS + XR * q
            pool.wait_ge(e("a_scan"), h + 1)
            for i in range(8):
                kk = (4 * h + q) * 8 + i
                if kk >= 2:
                    pool.wait_ge(e("d_used"), kk - 1)
                dd = DD[:, kk % 2]
                if i < 7:
                    m = LEVELS[i]
                    bv = S["b"][:, c0:c0 + XR].rearrange("p (n two m) -> p n two m", two=2, m=m)
                    dv = dd.rearrange("p (n two m) -> p n two m", two=2, m=m)
                    ref = bv[:, :, 0, m - 1:m].to_broadcast([P, XR // (2 * m), m])
                    st(nc.gpsimd.tensor_tensor(dv[:, :, 0, :], ref, bv[:, :, 0, :], SUB))
                    st.fire(nc.gpsimd.tensor_tensor(dv[:, :, 1, :], bv[:, :, 1, :], ref, SUB), e("d_ready"))
                else:
                    bv = S["b"][:, c0:c0 + XR].rearrange("p (n m) -> p n m", m=P)
                    ref = bv[:, :, P - 1:P].to_broadcast([P, XR // P, P])
                    st.fire(nc.gpsimd.tensor_tensor(dd.rearrange("p (n m) -> p n m", m=P), ref, bv, SUB), e("d_ready"))

        for h in range(5):
            later = U_A + 2 * h + 2 if h < 3 else U_B
            splits = {6: (later, 0), 8: (later, 1)}
            if h:
                splits.update({1: (U_A + 2 * h + 1, 0), 3: (U_A + 2 * h + 1, 1)})
            for kind, i in a_items(h):
                if kind == "F":
                    differences(h - 1, 0)
                if kind == "R" and i % 2 == 0 and i < 6:
                    differences(h - 1, i // 2 + 1)
                if kind == "P" and i in splits:
                    split_half(*splits[i])
        split_unit(U_B + 1)
        for j in range(4):
            if j == 0:
                pool.wait_ge(e("a_free"), 4)
                st.fire(nc.gpsimd.memset(GWB, 0.0), e("gw_zero"))
            if j < 2:
                split_unit(U_B + 2 + j)
        for u in range(U_M, U_O + 4):
            split_unit(u)

    @block.tensor
    def _(pe):
        mm = nc.tensor.matmul

        def split_product(out, wt, ht, ks, wcols, hcols, w_is_lhs):
            last = None
            n = len(ks)
            for i, k in enumerate(ks):
                for j, (x, y) in enumerate(((0, 0), (0, 1), (1, 0))):
                    wa, ha = wt[x][:, k, wcols], ht[y][:, k, hcols]
                    l, r = (wa, ha) if w_is_lhs else (ha, wa)
                    last = mm(out, lhsT=l, rhs=r, start=(i == 0 and j == 0), stop=(i == n - 1 and j == 2))
            return last

        def weights(u):
            pe.wait_ge(half_split, halves_before[u + 1])

        def drain(*rings):
            for r in rings:
                if r.p:
                    pe.wait_ge(r.free, r.p)

        pe.wait_ge(ld["g"], (2 + 1 + 7 + 2) * 16)
        nc.tensor.transpose(ps[:, 7, 0:60], PRMR, ID[0:60, 0:60])
        for j in range(4):
            nc.tensor.transpose(ps[:, 7, 64 + 32 * j:96 + 32 * j], CSTR[:, P * j:P * j + P], ID[0:32, 0:32])
        for k in range(8):
            last = nc.tensor.transpose(ps[:, 7, 192 + 9 * k:201 + 9 * k], C9[:, P * k:P * k + P], ID[0:9, 0:9])
        last.then_inc(e("cols_psum"), 1)
        pe.wait_ge(e("ct_ready"), 1)
        def modulation(i):
            pe.wait_ge(adw_in[i % 4], 16 * (i // 4 + 1))
            if i == 8:
                pe.wait_ge(e("mod_ready"), 1)
            for j in (2 * i, 2 * i + 1):
                for k in range(8):
                    last = mm(ps[:, 6, 9 * j:9 * j + 9], lhsT=ADW[:, i % 4, k, P * (j % 2):P * (j % 2) + P],
                              rhs=CT[:, k, :], start=(k == 0), stop=(k == 7))
            last.then_inc(e("ada_used"), 1)

        for i in range(8):
            modulation(i)
        pe.wait_ge(ld["x"], 9 * 16)
        for d in range(8):
            dc = slice(P * d, P * d + P)
            last = nc.tensor.transpose(ps[:, 7, 320 + 8 * d:328 + 8 * d], XS[:, dc], ID[0:8, 0:8])
        last.then_inc(e("cols_psum"), 1)
        for d in range(8):
            dc = slice(P * d, P * d + P)
            for hf in range(2):
                b = act3.acquire(pe)
                for t in range(4):
                    last = nc.tensor.transpose(ps[:, b, P * t:P * t + P], XIN[:, 4 * hf + t, dc], ID)
                last.then_inc(act3.full, 1)
        for i in range(8, 12):
            modulation(i)
        drain(act3)
        pe.wait_ge(e("h_ready"), 1)

        def tok_cols(t):
            return slice(0, P) if t == 0 else slice(NS + P * (t - 1), NS + P * t)

        def transpose_q(t):
            pe.wait_ge(e("q_tok"), t)
            b = tq.acquire(pe)
            for i in range(4):
                last = nc.tensor.transpose(ps[:, 4 + b, P * i:P * i + P], QTOK[:, P * i:P * i + P], ID)
            last.then_inc(tq.full, 1)
            pe.wait_ge(e("q_roped"), t)
            b = tr.acquire(pe)
            for i in range(4):
                last = nc.tensor.transpose(ps[:, 6 + b, P * i:P * i + P], QRTOK[:, P * i:P * i + P], ID)
            last.then_inc(tr.full, 1)

        weights(1)
        for t in range(9):
            b = p1.acquire(pe)
            for half in range(2):
                last = split_product(ps[:, b, 256 * half:256 * half + 256], wslot(half), H, range(8),
                                     slice(0, 256), tok_cols(t), False)
            last.then_inc(p1.full, 1)
            if t >= 2:
                transpose_q(t - 1)
        pe.wait_ge(p1.full, 9)
        pe.sem_inc(w_used, 2)
        transpose_q(8)

        def transpose_k(u, t):
            if u == 2:
                pe.wait_ge(e("kv_tok"), t)
                b = tq.acquire(pe)
                for i in range(2):
                    last = nc.tensor.transpose(ps[:, 4 + b, P * i:P * i + P], KV[:, t - 1, P * i:P * i + P], ID)
                last.then_inc(tq.full, 1)
            else:
                c = 256 if u == 3 else 512
                pe.wait_ge(e("k_roped"), 8 * (u - 3) + t)
                b = tr.acquire(pe)
                nc.tensor.transpose(ps[:, 6 + b, 0:P], KV[:, t - 1, c:c + P], ID).then_inc(tr.full, 1)

        for u in range(2, 6):
            weights(u)
            width = UNITS[u][1][0][1]
            for t in range(9):
                b = p1.acquire(pe)
                last = split_product(ps[:, b, 0:width], wslot(u), H, range(8), slice(0, width), tok_cols(t), False)
                last.then_inc(p1.full, 1)
                if t >= 2 and u < 5:
                    transpose_k(u, t - 1)
            pe.wait_ge(p1.full, p1.p)
            pe.sem_inc(w_used, 1)
            if u < 5:
                transpose_k(u, 8)
        drain(p1, tq, tr)
        pe.wait_ge(ld["w1"], (4 + 4 + 2) * 16)
        nc.tensor.transpose(ps[:, 0, 0:64], POSR.rearrange("p h d -> p (h d)"), ID[0:64, 0:64]).then_inc(e("cmp_psum"), 1)
        pe.wait_ge(e("cmp_sbuf"), 1)
        for c in range(2):
            for j in range(32):
                last = mm(ps[:, 0, 64 + c:65 + c], lhsT=W1B[:, c, j, :], rhs=POST[:, 32 * c + j:32 * c + j + 1],
                          start=(j == 0), stop=(j == 31))
        last.then_inc(e("cmp_psum"), 1)
        for c in range(2):
            for j in range(32):
                last = mm(ps[:, 1 + c, 0:NCMP], lhsT=W1B[:, c, j, :], rhs=KTT[:, c, j:j + 16 * (NCMP - 1) + 1:16],
                          start=(j == 0), stop=(j == 31))
            last.then_inc(e("hid"), 1)
        pe.wait_ge(e("hid_gelu"), 2)
        mm(ps[:, 3, 0:P], lhsT=W2B[:, 0, :], rhs=HKV[:, 0, :], start=True, stop=True)
        mm(ps[:, 3, P:2 * P], lhsT=HKV[:, 1, :], rhs=W2B[:, 1, :], start=True, stop=True).then_inc(e("cmp_psum"), 1)
        pe.wait_ge(e("cmp_sbuf"), 3)

        groups = []
        gi = {}
        for u, (k, t, hh, g, k0, n) in enumerate(AU):
            if (t, k) not in gi:
                gi[(t, k)] = len(groups)
                groups.append(u)
            groups[gi[(t, k)]] = u

        def scores(u):
            k, t, hh, g, k0, n = AU[u]
            if u >= 2:
                pe.wait_ge(e("p_exp"), u - 1)
            s = 2 * (u % 2)
            tc = slice(P * t, P * t + P)
            if k == 0:
                for i in range(4):
                    last = mm(ps[:, s, P * i:P * i + P], lhsT=QT[:, i, tc], rhs=KCB, start=True, stop=True)
            else:
                gp = slice(64 * g, 64 * g + 64)
                for c in range(0, n, 4):
                    w = min(4, n - c)
                    last = mm(ps[:, s + c // 4, 0:P * w], lhsT=QRT[gp, hh, tc],
                              rhs=KTT[gp, 1 + k, P * (k0 + c):P * (k0 + c + w)], start=True, stop=True)
            last.then_inc(e("scored"), 1)

        acnt = [0, 0]

        def transposes(u):
            k, t, hh, g, k0, n = AU[u]
            pe.wait_ge(e("p_exp"), u + 1)
            for c in range(0, n, 4):
                rg = ta if c == 0 else tv
                rg.acquire(pe)
                bank = 4 if c == 0 else 5
                for i in range(min(4, n - c)):
                    last = nc.tensor.transpose(ps[:, bank, P * i:P * i + P], PR[:, u % 3, P * (c + i):P * (c + i) + P], ID)
                last.then_inc(rg.full, 1)
            need.append((ta.p, tv.p))

        need = []

        def pv(u):
            k, t, hh, g, k0, n = AU[u]
            oi = gi[(t, k)]
            pe.wait_ge(ta.free, need[u][0])
            if need[u][1]:
                pe.wait_ge(tv.free, need[u][1])
            if oi >= 2:
                pe.wait_ge(e("o_used"), oi - 1)
            bank = 6 + oi % 2
            if k == 0:
                for i in range(4):
                    last = mm(ps[:, bank, P * i:P * i + P], lhsT=PT[:, u % 2, P * i:P * i + P], rhs=VCB, start=True, stop=True)
            else:
                vc = (384 if k == 1 else 640) + 64 * g
                for i in range(n):
                    last = mm(ps[:, bank, P * hh + 64 * g:P * hh + 64 * g + 64], lhsT=PT[:, u % 2, P * i:P * i + P],
                              rhs=KV[:, k0 + i, vc:vc + 64], start=(i == 0), stop=(i == n - 1))
            last.then_inc(e("pv_done"), 1)

        scores(0)
        NU = len(AU)
        for u in range(NU + 1):
            if u + 1 < NU:
                scores(u + 1)
            if u < NU:
                transposes(u)
            if u >= 1:
                pv(u - 1)
        pe.wait_ge(e("s4_start"), 1)
        for x, src in ((0, CS[:, 0:512]), (1, CSR)):
            mm(ps[0:64, x, :], lhsT=G[0:8, GE8:GE8 + 64], rhs=src, start=True, stop=True).then_inc(e("q_exp"), 1)
        pe.wait_ge(e("q_rows"), 1)
        for x in range(2):
            nc.tensor.transpose(ps[:, 2, 64 * x:64 * x + 64], QROW[:, x, :], ID[0:64, 0:64])
        nc.tensor.transpose(ps[:, 2, 128:136], CS[:, 768:896], ID[0:8, 0:8]).then_inc(e("q_cols"), 1)
        pe.wait_ge(e("q_bd"), 1)
        pe.wait_ge(ld["w1"], (8 + 2 + 4) * 16)

        def page_transposes(b, groups):
            s = b % 2
            if 0 in groups:
                pe.wait_ge(pgc_in[s], 16 * 16 * (b // 2 + 1))
            if 4 in groups:
                pe.wait_ge(pg_in[s], (8 + 4) * 16 * (b // 2 + 1))
            srcs = [(PGC, P * i, 0) for i in range(4)] + [(PG, 0, 0), (PG, 0, 4), (WR, 0, 0)]
            for i in groups:
                buf, c, j0 = srcs[i]
                rg, bank = (sa, 0) if i % 2 == 0 else (sv, 2)
                q = rg.acquire(pe)
                for j in range(4):
                    last = nc.tensor.transpose(ps[:, bank + q, P * j:P * j + P], buf[:, s, j0 + j, c:c + P], ID)
                last.then_inc(rg.full, 1)

        def hidden(b):
            pe.wait_ge(sa.free, 4 * b + 2)
            pe.wait_ge(sv.free, 3 * b + 2)
            if b:
                pe.wait_ge(e("s_gelu"), b)
            for c in range(2):
                for j in range(16):
                    last = mm(ps[0:64, 3, 128 * c:128 * c + 2 * NCMP], lhsT=W1S[:, c, j, :],
                              rhs=CMT[:, c, :, j:j + 8 * (NCMP - 1) + 1:8], start=(j == 0), stop=(j == 15))
            last.then_inc(e("s_hid"), 1)

        page_transposes(0, range(7))
        hidden(0)
        for b in range(NS):
            s = b % 2
            qr = QBD[:, 1, 8 * b:8 * b + 8]
            more = b + 1 < NS
            pe.wait_ge(sa.free, 4 * b + 4)
            pe.wait_ge(sv.free, 3 * b + 3)
            for c in range(2):
                mm(ps[0:8, 4 + c, :], lhsT=qr, rhs=KST[:, 512 * c:512 * c + 512], start=True, stop=True)
            if b:
                pe.wait_ge(e("s_ots"), b)
            mm(ps[0:8, 6, :], lhsT=qr, rhs=KWT, start=True, stop=True).then_inc(e("s_scored"), 1)
            pe.wait_ge(e("s_gelu"), b + 1)
            for g in range(2):
                gc = slice(NCMP * g, NCMP * g + NCMP)
                mm(ps[64 * g:64 * g + 64, 7, 128:128 + NCMP], lhsT=W2S[:, 0, :], rhs=HKS[:, 0, gc], start=True, stop=True)
                last = mm(ps[0:NCMP, 7, 192 + 64 * g:256 + 64 * g], lhsT=HKS[:, 1, gc], rhs=W2S[:, 1, :], start=True, stop=True)
            last.then_inc(e("s_kcvc"), 1)
            if more:
                page_transposes(b + 1, (0, 1))
            pe.wait_ge(e("s_kcvc_ready"), b + 1)
            mm(ps[0:8, 7, 320:320 + NCMP], lhsT=QBD[:, 0, 8 * b:8 * b + 8], rhs=KCS[:, 0:NCMP], start=True, stop=True).then_inc(e("s_cmps"), 1)
            if more:
                page_transposes(b + 1, (2, 3))
            pe.wait_ge(e("s_imp_in"), b + 1)
            mm(ps[0:8, 7, 400:401], lhsT=qr, rhs=NKT[:, b:b + 1], start=True, stop=True)
            mm(ps[0:8, 7, 384:400], lhsT=G[0:8, GG8:GG8 + 8], rhs=SEL[:, 0:16], start=True, stop=True).then_inc(e("s_imp"), 1)
            if more:
                page_transposes(b + 1, (4, 5, 6))
                hidden(b + 1)
            pe.wait_ge(e("s_norm"), b + 1)
            nc.tensor.transpose(ps[0:NCMP, 7, 404:412], PCS[:, 1:1 + NCMP], ID[0:8, 0:8])
            for i in range(8):
                nc.tensor.transpose(ps[:, 7, 412 + 8 * i:420 + 8 * i], SRW[:, P * i:P * i + P], ID[0:8, 0:8])
            nc.tensor.transpose(ps[0:1, 7, 476:484], SRW[:, 1024:1025], ID[0:8, 0:8])
            for i in range(3):
                nc.tensor.transpose(ps[:, 7, 484 + 8 * i:492 + 8 * i], PW8[:, P * i:P * i + P], ID[0:8, 0:8])
            nc.tensor.transpose(ps[:, 6, 0:8], PW8[:, 384:512], ID[0:8, 0:8]).then_inc(e("s_pt"), 1)
            pe.wait_ge(e("s_pts"), b + 1)
            mm(ps[:, 6, 8:16], lhsT=VCS[0:NCMP, :], rhs=PTS[0:NCMP, 0:8], start=True, stop=True)
            for i in range(8):
                mm(ps[:, 6, 16:24], lhsT=PG[:, s, i, P:2 * P], rhs=PTS[:, 8 + 8 * i:16 + 8 * i], start=(i == 0), stop=False)
            mm(ps[:, 6, 16:24], lhsT=NVR[:, s, :], rhs=PTS[0:1, 72:80], start=False, stop=True)
            for i in range(4):
                last = mm(ps[:, 6, 24:32], lhsT=WR[:, s, i, P:2 * P], rhs=PTS[:, 80 + 8 * i:88 + 8 * i], start=(i == 0), stop=(i == 3))
            last.then_inc(e("s_pv"), 1)
        pe.wait_ge(e("s_ots"), NS)

        weights(U_CZ + 1)
        for t in range(9):
            b = pz.acquire(pe)
            for half in range(2):
                last = split_product(ps[:, b, 256 * half:256 * half + 256], wslot(U_CZ + half), H, range(8),
                                     slice(0, 256), tok_cols(t), False)
            last.then_inc(pz.full, 1)
            if t >= 2:
                yc_transposes(pe, t - 1)
        pe.wait_ge(pz.full, 9)
        pe.sem_inc(w_used, 2)
        yc_transposes(pe, 8)
        pe.wait_ge(e("cs_cz"), 1)
        mm(ps[0:64, 6, 0:512], lhsT=G[0:8, GE8:GE8 + 64], rhs=CS[:, 1304:1816], start=True, stop=True)
        mm(ps[0:64, 7, 0:24], lhsT=G[0:8, GE8:GE8 + 64], rhs=CS[:, 1280:1304], start=True, stop=True)
        for i in range(3):
            last = nc.tensor.transpose(ps[0:64, 7, 32 + P * i:32 + P * i + P], OTS[:, i, :], ID)
        last.then_inc(e("f_psum"), 1)
        pe.wait_ge(e("f_sbuf"), 2)
        for i in range(4):
            last = mm(ps[:, 7, 416 + 8 * i:424 + 8 * i], lhsT=YSM[:, P * i:P * i + P], rhs=G[0:64, GE64:GE64 + 8], start=True, stop=True)
        last.then_inc(e("f_psum"), 1)
        pe.wait_ge(e("yc_done"), 1)

        drain(pz, tz)

        def feature_group(rg, bank0, wt, wcols):
            for c in range(3):
                b = rg.acquire(pe)
                last = split_product(ps[:, bank0 + b, 0:CH], wt, H, range(8), wcols, slice(CH * c, CH * c + CH), True)
                last.then_inc(rg.full, 1)

        def a_group(h, i):
            u = U_A + 2 * h + i // 6
            if i % 6 == 0:
                weights(u)
            if i in (0, 1, 2, 9, 10, 11):
                b, rg = pq.acquire(pe), pq
                last = split_product(ps[:, b, 0:CH], wslot(u), H, range(8), slice(0, P) if i < 3 else slice(P, 2 * P),
                                     slice(CH * (i % 3), CH * (i % 3) + CH), True)
            elif i < 6:
                b, rg = pf.acquire(pe), pf
                last = split_product(ps[:, 3 + b, 0:CH], wslot(u), H, range(8), slice(P, 2 * P),
                                     slice(CH * (i % 3), CH * (i % 3) + CH), True)
            else:
                b, rg = pf.acquire(pe), pf
                for x, t in enumerate(([0], [1, 2, 3, 4], [5, 6, 7, 8])[i - 6]):
                    last = split_product(ps[:, 3 + b, P * x:P * x + P], wslot(u), H, range(8), slice(0, P), tok_cols(t), False)
            last.then_inc(rg.full, 1)
            if i % 6 == 5:
                pe.wait_ge(rg.full, rg.p)
                pe.sem_inc(w_used, 1)

        natt = [0]

        def a_levels(h, c):
            S = AS[h % 2]
            q = 4 * h + c // 2
            pe.wait_ge(e("x_ready"), q + 1)
            if natt[0]:
                pe.wait_ge(e("att_masked"), natt[0])
            natt[0] += 1
            cc = slice(P * (c % 2), P * (c % 2) + P)
            tc = slice(NS + P * c, NS + P * c + P)
            for i in range(7):
                x = XQ[:, q % 2, i, cc]
                mm(ps[:, 5 + i // 4, P * (i % 4):P * (i % 4) + P], lhsT=x, rhs=x, start=True, stop=True)
            mm(ps[:, 6, 384:512], lhsT=S["k"][:, tc], rhs=S["q"][:, tc], start=True, stop=True).then_inc(e("att_full"), 1)
            i = 8 * h + c
            if i >= 1:
                pe.wait_ge(e("kot_ready"), i)
            nc.tensor.transpose(ps[:, 2, 0:P], XQ[:, q % 2, 8, cc], ID).then_inc(e("kot_full"), 1)

        def a_output(h, c):
            S = AS[h % 2]
            q = 4 * h + c // 2
            i = 8 * h + c
            cc = slice(P * (c % 2), P * (c % 2) + P)
            pe.wait_ge(e("att_ready"), i + 1)
            pe.wait_ge(e("kot_ready"), i + 1)
            if i:
                pe.wait_ge(e("s_ready"), i)
            if c == 3:
                pe.wait_ge(e("os_read"), h + 1)
            mm(ps[:, 7, P:2 * P], lhsT=S["v"][:, c, :], rhs=ATT[:, i % 2], start=True, stop=(c == 0))
            if c:
                mm(ps[:, 7, P:2 * P], lhsT=STA, rhs=XQ[:, q % 2, 7, cc], start=False, stop=True)
            mm(ps[:, 7, 2 * P:3 * P], lhsT=KOT[:, i % 2], rhs=S["v"][:, c, :], start=True, stop=True).then_inc(e("chunk_full"), 1)

        def a_sample(h):
            S = AS[h % 2]
            if natt[0]:
                pe.wait_ge(e("att_masked"), natt[0])
            natt[0] += 1
            for b in range(NS):
                last = mm(ps[:, 5 + b // 4, P * (b % 4):P * (b % 4) + P], lhsT=ID[0:8, b:b + 1].to_broadcast([8, P]),
                          rhs=S["vs"], start=True, stop=True)
            last.then_inc(e("att_full"), 1)
            pe.wait_ge(e("sts_done"), h + 1)
            pe.wait_ge(e("s_ready"), 8 * h + 3)
            for b in range(NS):
                last = mm(ps[:, 7, 384 + b:385 + b], lhsT=STS[:, b, :], rhs=S["q"][:, b:b + 1], start=True, stop=True)
            last.then_inc(e("os_full"), 1)

        def a_norm(h):
            for c in range(3):
                b = pf.acquire(pe)
                if c == 0:
                    pe.wait_ge(e("sq_ready"), h + 1)
                mm(ps[:, 3 + b, 0:CH], lhsT=ONES, rhs=YA[:, CH * c:CH * c + CH], start=True, stop=True).then_inc(pf.full, 1)

        projected = []
        for h in range(5):
            if h:
                pe.wait_ge(pq.free, projected[h - 1][0])
                pe.wait_ge(pf.free, projected[h - 1][1])
            for kind, i in a_items(h):
                if kind == "P":
                    a_group(h, i)
                elif kind == "S":
                    a_sample(h - 1)
                elif kind == "R":
                    a_levels(h - 1, i)
                    if i:
                        a_output(h - 1, i - 1)
                    if i == 7:
                        a_output(h - 1, 7)
                elif kind == "N":
                    a_norm(h - 1)
            projected.append((pq.p, pf.p))

        drain(pq, pf)
        act3.restart_filling(3)
        ta.restart_filling(3)
        pe.wait_ge(e("chunk_full"), 32)
        pe.wait_ge(e("s_ready"), 32)

        def columns_out(j):
            pe.wait_ge(e("oc_cols"), j + 1)
            nc.tensor.transpose(ps[0:20, 6, P * j:P * j + P], OCO[:, j % 2, 0:20], ID).then_inc(e("oc_rows"), 1)

        for j in range(5):
            if j < 4:
                weights(U_B + j)
                feature_group(act3, 0, wslot(U_B + j), slice(0, P))
            if j:
                pe.wait_ge(gw_in[(j - 1) % 2], 64 * ((j + 1) // 2))
                pe.wait_ge(e("u_ready"), j)
                for x in range(2):
                    for c in range(3):
                        b = ta.acquire(pe)
                        last = mm(ps[:, 3 + b, 0:CH], lhsT=GWB[:, (j - 1) % 2, x, :], rhs=BU[:, (j - 1) % 2, CH * c:CH * c + CH],
                                  start=True, stop=True)
                        last.then_inc(ta.full, 1)
            if j < 4:
                feature_group(act3, 0, wslot(U_B + j), slice(P, 2 * P))
                pe.wait_ge(act3.full, act3.p)
                pe.sem_inc(w_used, 1)
            if j >= 2:
                columns_out(j - 2)
        columns_out(3)
        drain(act3, ta)
        act3.restart_filling(4)
        tv.restart_filling(4)
        for m in range(3):
            for dp in range(4):
                u = U_M + 8 * m + 2 * dp
                weights(u)
                for i in range(2):
                    feature_group(act3, 0, wslot(u), slice(P * i, P * i + P))
                    if i == 0:
                        continue
                    pe.wait_ge(act3.full, act3.p)
                    pe.sem_inc(w_used, 1)
                    weights(u + 1)
                    if dp == 0:
                        pe.wait_ge(e("y_split"), m + 1)
                    for x in range(2):
                        for c in range(3):
                            b = tv.acquire(pe)
                            last = split_product(ps[:, 4 + b, 0:CH], wslot(u + 1), YH, range(4), slice(P * x, P * x + P),
                                                 slice(CH * c, CH * c + CH), True)
                            last.then_inc(tv.full, 1)
                pe.wait_ge(tv.full, tv.p)
                pe.sem_inc(w_used, 1)
                if dp == 3:
                    pe.sem_inc(e("y_used"), 1)
        drain(act3, tv)
        tv.restart_filling(4)
        for j in range(8):
            last = nc.tensor.transpose(ps[0:9, 6 + j // 4, P * (j % 4):P * (j % 4) + P], MOD[:, 16 + j, :], ID)
        last.then_inc(e("gate_psum"), 1)
        pe.wait_ge(e("gate_sbuf"), 1)
        for q in range(2):
            last = mm(ps[:, 4 + q, :], lhsT=ID[0:9, 8:9].to_broadcast([9, P]), rhs=GSR[:, 512 * q:512 * q + 512], start=True, stop=True)
        last.then_inc(e("gate_psum"), 1)
        pe.wait_ge(e("gate_sbuf"), 2)
        pe.wait_ge(e("acc_split"), 1)
        for t in range(9):
            for q in range(4):
                if t == 0:
                    weights(U_O + q)
                if q % 2 == 0:
                    b = tv.acquire(pe)
                last = split_product(ps[:, b, 256 * (q % 2):256 * (q % 2) + 256], wslot(U_O + q), H, range(8), slice(0, 256), tok_cols(t), False)
                if q % 2:
                    last.then_inc(tv.full, 1)

    @block.scalar
    def _(act):
        st = Steps(act, own["act"])
        A = nc.scalar.activation
        CP = ACT.Copy
        act.wait_ge(e("ct_ready"), 1)
        st(A(LN[:, 16:20], PRM[:, 56:60], ACT.Abs))
        st(A(LN[:, 16:20], LN[:, 16:20], ACT.Exp, scale=-1.0))
        st(A(LN[:, 16:20], LN[:, 16:20], ACT.Ln, bias=1.0), e("lam_ln"))
        act.wait_ge(e("mod_ready"), 1)
        for d in range(8):
            s = hraw_ring.acquire(act)
            for hf in range(2):
                b = act3.take(act)
                st(A(HRAW[:, s, 512 * hf:512 * hf + 512], ps[:, b, :], ACT.Identity, bias=MOD[:, d, 8:9], scale=MOD[:, 8 + d, 8:9]), act3.free)
            st.mark(hraw_ring.full)
        for t in range(9):
            b = p1.take(act)
            if t == 0:
                st(A(CS[:, 0:512], ps[0:8, b, :], CP), p1.free)
            else:
                if t == 1:
                    act.wait_ge(e("h_ready"), 1)
                if t >= 2:
                    act.wait_ge(e("q_roped"), t - 1)
                    act.wait_ge(tq.full, t - 1)
                src = ps[:, b, :].rearrange("p (g h d) -> p g h d", g=2, h=4)
                dst = QTOK.rearrange("p (h g d) -> p g h d", g=2, h=4)
                st(A(dst, src, CP), e("q_tok"))
                st.mark(p1.free)
            if t >= 2:
                q = tq.take(act)
                st(A(QT[:, :, P * (t - 2):P * (t - 1)], ps[:, 4 + q, :].rearrange("p (h c) -> p h c", h=4), CP), tq.free)
        q = tq.take(act)
        st(A(QT[:, :, P * 7:P * 8], ps[:, 4 + q, :].rearrange("p (h c) -> p h c", h=4), CP), tq.free)

        def k_out(t):
            q = tq.take(act)
            st(A(KTT[:, 0:2, P * (t - 1):P * t], ps[:, 4 + q, 0:256].rearrange("p (h c) -> p h c", h=2), CP), tq.free)

        for u in range(2, 6):
            width = UNITS[u][1][0][1]
            c = (u - 2) * 256
            for t in range(9):
                b = p1.take(act)
                if t == 0:
                    st(A(CS[:, 512 + c:512 + c + width], ps[0:8, b, 0:width], CP), p1.free)
                elif u < 5:
                    st(A(KV[:, t - 1, c:c + 256], ps[:, b, 0:256], CP), e("kv_tok"))
                    st.mark(p1.free)
                else:
                    st(A(G3[:, t - 1, :], ps[:, b, 0:24], ACT.Sigmoid), p1.free)
                if u == 2 and t >= 2:
                    k_out(t - 1)
            if u == 2:
                k_out(8)
        act.wait_ge(e("cmp_sbuf"), 2)
        for c in range(2):
            act.wait_ge(e("hid"), c + 1)
            for h in range(2):
                hp = slice(64 * h, 64 * h + 64)
                ins = A(HKV[hp, c, 64 * h:64 * h + NCMP], ps[hp, 1 + c, 0:NCMP], ACT.Gelu_apprx_tanh, bias=PB[hp, c:c + 1])
                st(ins, e("hid_gelu") if h else None)
        def exps(u):
            k, t, hh, g, k0, n = AU[u]
            act.wait_ge(e("nm_ready"), u + 1)
            if u >= 3:
                act.wait_ge(e("pv_done"), u - 2)
            if k == 0:
                st(A(PR[:, u % 3, 0:512], SC, ACT.Exp, scale=SCALE), e("p_exp"))
            else:
                s = 2 * (u % 2)
                src = ps[:, s:s + 2, :].rearrange("p b c -> p (b c)")[:, 0:P * n]
                st(A(PR[:, u % 3, 0:P * n], src, ACT.Exp, bias=NM[:, u % 4:u % 4 + 1], scale=SCALE,
                     accum_out=SM[:, t % 2, 8 * k + 2 * hh + g:8 * k + 2 * hh + g + 1]), e("p_exp"))

        def ta_out(u):
            n = min(4, AU[u][5])
            ta.take(act)
            if u >= 2:
                act.wait_ge(e("pv_done"), u - 1)
            st(A(PT[:, u % 2, 0:P * n], ps[:, 4, 0:P * n], CP), ta.free)

        exps(0)
        for u in range(len(AU)):
            ta_out(u)
            if u + 1 < len(AU):
                exps(u + 1)
        dsts = [CMT[:, 0, 0, :], CMT[:, 1, 0, :], KST[:, 0:512], KWT]
        act.wait_ge(e("q_bd"), 1)

        def keys_out(b, i):
            if b and i == 0:
                act.wait_ge(e("s_hid"), b)
            if b and i == 2:
                act.wait_ge(e("s_scored"), b)
            q = sa.take(act)
            st(A(dsts[i], ps[:, q, :], CP), sa.free)

        for i in range(4):
            keys_out(0, i)
        for b in range(NS):
            act.wait_ge(e("s_hid"), b + 1)
            if b:
                act.wait_ge(e("s_kcvc"), b)
            for c in range(2):
                st(A(HKS[:, c, :], ps[0:64, 3, 128 * c:128 * c + 2 * NCMP], ACT.Gelu_apprx_tanh, bias=PB[0:64, c:c + 1]), e("s_gelu") if c else None)
            if b + 1 < NS:
                keys_out(b + 1, 0)
            act.wait_ge(e("s_m0"), b + 1)
            st(A(PCS[:, 1:1 + NCMP], ps[0:8, 7, 320:320 + NCMP], ACT.Exp, bias=SM8[:, 0:1], scale=SCALE, accum_out=SM8[:, 3:4]), e("s_e0"))
            if b + 1 < NS:
                for i in (1, 2, 3):
                    keys_out(b + 1, i)
            act.wait_ge(e("s_m1"), b + 1)
            st(A(SRW[:, 0:1025], SRW[:, 0:1025], ACT.Exp, bias=SM8[:, 1:2], scale=SCALE, accum_out=SM8[:, 4:5]), e("s_exp"))
            st(A(PW8, ps[0:8, 6, :], ACT.Exp, bias=SM8[:, 2:3], scale=SCALE, accum_out=SM8[:, 5:6]), e("s_exp"))
        for t in range(9):
            b = pz.c % 4
            act.wait_ge(pz.full, t + 1)
            if t == 0:
                st(A(CS[:, 1304:1816], ps[0:8, 0, :], CP), e("cs_cz"))
            else:
                if t >= 3:
                    act.wait_ge(e("yc_tok"), t - 2)
                st(A(SGZ[:, t % 2, :], ps[:, t % 4, :], ACT.Sigmoid), e("z_sig"))
            if t >= 2:
                yc_out(act, st, t - 1)
        yc_out(act, st, 8)
        act.wait_ge(e("f_psum"), 1)
        st(A(CGX, ps[0:64, 7, 0:24], ACT.Sigmoid), e("f_sig"))
        act.wait_ge(e("f_sbuf"), 1)
        st(A(CZ2, CZ1, ACT.Sigmoid), e("f_sig"))
        def a_group(h, i):
            S = AS[h % 2]
            c = i % 3
            cc = slice(CH * c, CH * c + CH)
            if i < 3 or i >= 9:
                n = 6 * h + (i if i < 3 else i - 6)
                act.wait_ge(pq.full, n + 1)
                if i == 0:
                    act.wait_ge(e("a_start"), 1)
                    if h >= 2:
                        act.wait_ge(e("ya_done"), h - 1)
                if i == 9:
                    act.wait_ge(e("a_lf"), h + 1)
                st(A(SGA[:, cc], ps[:, n % 2, 0:CH], ACT.Sigmoid), e("sg_ready"))
            elif i < 6:
                if i == 3:
                    act.wait_ge(pq.free, 6 * h + 3)
                b = pf.take(act)
                st(A(S["k"][:, cc], ps[:, 3 + b, 0:CH], ACT.Sigmoid, scale=-1.0))
                st(A(S["b"][:, cc], ps[:, 3 + b, 0:CH], CP))
                st(A(SGA[:, cc], ps[:, 3 + b, 0:CH], ACT.Abs), pf.free)
                if i == 5:
                    st(A(SGA, SGA, ACT.Exp, scale=-1.0))
                    st(A(SGA, SGA, ACT.Ln, bias=1.0), e("sp_ready"))
            else:
                b = pf.take(act)
                if i == 6:
                    st(A(S["vs"], ps[0:8, 3 + b, 0:P], CP), pf.free)
                else:
                    st(A(S["v"][:, 4 * (i - 7):4 * (i - 6), :], ps[:, 3 + b, :].rearrange("p (t v) -> p t v", t=4), CP), pf.free)

        def a_exps(h, q):
            S = AS[h % 2]
            c0 = NS + XR * q
            qq = 4 * h + q
            act.wait_ge(e("a_scan"), h + 1)
            for i in range(8):
                kk = qq * 8 + i
                act.wait_ge(e("d_ready"), kk + 1)
                st(A(DD[:, kk % 2], DD[:, kk % 2], ACT.Exp), e("d_exp"))
            if qq >= 2:
                act.wait_ge(e("s_ready"), 2 * (qq - 1))
            st(A(XQ[:, qq % 2, 7, :], S["b"][:, c0:c0 + XR], ACT.Exp))
            bl = S["b"][:, c0:c0 + XR].rearrange("p (n m) -> p n m", m=P)[:, :, P - 1:P]
            st(A(EL[:, qq % 2, :].rearrange("p (n o) -> p n o", o=1), bl, ACT.Exp), e("eb_ready"))

        def a_key(i):
            act.wait_ge(e("kot_full"), i + 1)
            if i >= 2:
                act.wait_ge(e("chunk_full"), i - 1)
            st(A(KOT[:, i % 2], ps[:, 2, 0:P], CP), e("kot_ready"))

        def a_norm(h):
            act.wait_ge(e("ot_ready"), h + 1)
            if h:
                act.wait_ge(e("a_free"), h)
            st(A(YA, OT, ACT.Square), e("sq_ready"))
            act.wait_ge(pq.free, min(6 * (h + 2), 24))
            for c in range(3):
                b = pf.take(act)
                st(A(SGA[:, CH * c:CH * c + CH], ps[:, 3 + b, 0:CH], ACT.Ln, bias=G[:, GEPS:GEPS + 1], scale=1.0 / P), pf.free)
            st(A(SGA, SGA, ACT.Exp, scale=-0.5), e("rms_ready"))

        for h in range(5):
            for kind, i in a_items(h):
                if kind == "P":
                    a_group(h, i)
                elif kind == "F":
                    a_exps(h - 1, 0)
                elif kind == "R":
                    a_key(8 * (h - 1) + i)
                    if i % 2 == 0 and i < 6:
                        a_exps(h - 1, i // 2 + 1)
                elif kind == "N":
                    a_norm(h - 1)
        act.wait_ge(e("prm8_ready"), 1)
        act3.restart_emptying(3)
        ta.restart_emptying(3)
        for j in range(5):
            if j < 4:
                for c in range(3):
                    b = act3.take(act)
                    if c == 0:
                        if j == 0:
                            act.wait_ge(e("a_free"), 4)
                        if j >= 2:
                            act.wait_ge(e("b_done"), j - 1)
                        st(A(BXP[:, j % 2, 0:8], ps[:, b, 0:8], CP))
                        st(A(BXP[:, j % 2, 11:3 + CH], ps[:, b, 8:CH], CP), act3.free)
                    else:
                        st(A(BXP[:, j % 2, 3 + CH * c:3 + CH * c + CH], ps[:, b, 0:CH], CP), act3.free)
                st.mark(e("bx_ready"))
            if j:
                jj = j - 1
                if jj:
                    act.wait_ge(e("b_done"), jj)
                for x, dst in ((0, BR), (1, BI)):
                    for c in range(3):
                        b = ta.take(act)
                        st(A(dst[:, CH * c:CH * c + CH], ps[:, 3 + b, 0:CH], ACT.Sigmoid, bias=PRM[:, 48 + 4 * x + jj:49 + 4 * x + jj]), ta.free)
                st(A(BA, BR, ACT.Exp, scale=C8[:, jj:jj + 1]))
                st(A(BT, BR, ACT.Tanh, scale=C8[:, 4 + jj:5 + jj]))
                st(A(BR, BT, ACT.Ln, bias=1.0))
                st(A(BR, BR, ACT.Exp, scale=-1.0), e("b_at"))
            if j < 4:
                for c in range(3):
                    b = act3.take(act)
                    st(A(BZ[:, j % 2, CH * c:CH * c + CH], ps[:, b, 0:CH], CP), act3.free)
            if j:
                act.wait_ge(e("b_om"), jj + 1)
                st(A(BT, BT, ACT.Sqrt, scale=2.0))
                st(A(BR, BZ[:, jj % 2, :], ACT.Sigmoid), e("b_sq"))
        act3.restart_emptying(4)
        n = 0
        for m in range(3):
            for dt in range(8):
                if n >= 2:
                    act.wait_ge(e("sg_used"), n - 1)
                if n == 0:
                    act.wait_ge(e("b_free"), 1)
                for c in range(3):
                    b = act3.take(act)
                    st(A(SGM[:, n % 2, CH * c:CH * c + CH], ps[:, b, 0:CH], ACT.Sigmoid), act3.free)
                st.mark(e("sgm_ready"))
                n += 1
        for t in range(9):
            act.wait_ge(e("var_ready"), t + 1)
            st(A(LN[:, 8 + t % 2:9 + t % 2], BAG[:, 1:2], ACT.Sqrt, bias=G[:, GEPS:GEPS + 1]), e("sd_ready"))

    @block.vector
    def _(v):
        st = Steps(v, own["dve"])
        V = nc.vector
        tt, ts, stt, cp = V.tensor_tensor, V.tensor_scalar, V.scalar_tensor_tensor, V.tensor_copy

        def bc(x, shape):
            return x.to_broadcast(shape)

        v.wait_ge(e("cols_psum"), 1)
        st(cp(PRM, ps[:, 7, 0:60]))
        st(cp(CST, ps[:, 7, 64:192].rearrange("p (j c) -> p j c", j=4)))
        st(cp(CT, ps[:, 7, 192:264].rearrange("p (k c) -> p k c", k=8)), e("ct_ready"))
        v.wait_ge(e("lam_ln"), 1)
        st(ts(LN[:, 20:24], PRM[:, 56:60], -1.0, 0.0, MUL, MAX))
        st(tt(LN[:, 20:24], LN[:, 20:24], LN[:, 16:20], ADD))
        st(V.tensor_scalar_mul(C8[:, 0:4], LN[:, 20:24], -LRU_C))
        st(V.tensor_scalar_mul(C8[:, 4:8], LN[:, 20:24], LRU_C), e("prm8_ready"))
        def modulation(part, n):
            v.wait_ge(e("ada_used"), n)
            js = slice(0, 16) if part == 0 else slice(16, 24)
            m = js.stop - js.start
            st(tt(MOD[:, js, :], ps[:, 6, 9 * js.start:9 * js.stop].rearrange("p (j c) -> p j c", c=9),
                  bc(PRM[:, js].unsqueeze(2), [P, m, 9]), ADD))
            if part == 0:
                st(V.tensor_scalar_add(MOD[:, 8:16, :], MOD[:, 8:16, :], 1.0), e("mod_ready"))
        modulation(0, 8)
        v.wait_ge(e("cols_psum"), 2)
        st(tt(HRS, ps[:, 7, 320:384].rearrange("p (d b) -> p d b", d=8), MOD[:, 8:16, 0:8], MUL))
        st(tt(HRS, HRS, MOD[:, 0:8, 0:8], ADD))
        st(cp(H[0][:, :, 0:8], HRS))
        st(tt(H[1][:, :, 0:8], HRS, Hf[0][:, :, 0:8], SUB))
        for d in range(8):
            s = hraw_ring.take(v)
            st(cp(H[0][:, d, NS:TC], HRAW[:, s, :]))
            st(tt(H[1][:, d, NS:TC], HRAW[:, s, :], Hf[0][:, d, NS:TC], SUB), hraw_ring.free)
        modulation(1, 12)
        st.mark(e("h_ready"))

        def rope(dst, src, tab, n, sem_, parts=P):
            x = src.rearrange("p (h d) -> p h d", d=HD)
            y = dst.rearrange("p (h d) -> p h d", d=HD)
            ta_ = RTA[0:parts, 0:64 * n].rearrange("p (h d) -> p h d", d=HD)
            tb_ = RTB[0:parts, 0:64 * n].rearrange("p (h d) -> p h d", d=HD)
            tab = tab.unsqueeze(1)
            st(tt(ta_, x, bc(tab[:, :, 0:64], [parts, n, 64]), MUL))
            st(tt(tb_, x, bc(tab[:, :, 64:128], [parts, n, 64]), MUL))
            st(tt(y[:, :, 0:32], ta_[:, :, 0:32], tb_[:, :, 32:64], ADD))
            st(tt(y[:, :, 32:64], ta_[:, :, 32:64], tb_[:, :, 0:32], ADD), sem_)

        def qr_out(t):
            q = tr.take(v)
            st(cp(QRT[:, :, P * (t - 1):P * t], ps[:, 6 + q, :].rearrange("p (h c) -> p h c", h=4)), tr.free)

        v.wait_ge(ld["cc"], 16)
        for t in range(1, 9):
            v.wait_ge(e("q_tok"), t)
            if t >= 2:
                v.wait_ge(tr.full, t - 1)
            tab = CC[:, P * (t - 1):P * t]
            rope(QRTOK[:, 0:256], QTOK[:, 0:256], tab, 4, None)
            rope(QRTOK[:, 256:512], QTOK[:, 256:512], tab, 4, e("q_roped"))
            if t >= 2:
                qr_out(t - 1)
        qr_out(8)
        for u in (3, 4):
            c = 256 * (u - 2)

            def kr_out(t):
                q = tr.take(v)
                st(cp(KTT[:, u - 1, P * (t - 1):P * t], ps[:, 6 + q, 0:P]), tr.free)
            for t in range(1, 9):
                v.wait_ge(e("kv_tok"), 8 * (u - 2) + t)
                rope(KV[:, t - 1, c:c + P], KV[:, t - 1, c:c + P], CC[:, P * (t - 1):P * t], 2, e("k_roped"))
                if t >= 2:
                    kr_out(t - 1)
            kr_out(8)
        tab = G[0:8, GRP:GRP + 128]
        rope(CSR[:, 0:256], CS[:, 0:256], tab, 4, None, 8)
        rope(CSR[:, 256:512], CS[:, 256:512], tab, 4, None, 8)
        rope(CS[:, 768:896], CS[:, 768:896], tab, 2, None, 8)
        rope(CS[:, 1024:1152], CS[:, 1024:1152], tab, 2, e("cs_roped"), 8)
        st.mark(e("kv_done"))
        v.wait_ge(e("cmp_psum"), 1)
        st(cp(POST, ps[:, 0, 0:64]), e("cmp_sbuf"))
        v.wait_ge(e("cmp_psum"), 2)
        st(cp(PB, ps[:, 0, 64:66]), e("cmp_sbuf"))
        v.wait_ge(e("cmp_psum"), 3)
        st(cp(KCB, ps[:, 3, 0:P]))
        st(cp(VCB, ps[:, 3, P:2 * P]), e("cmp_sbuf"))
        caus, edge = CC[:, 1536:1664], CC[:, 1664:1792]
        NU = len(AU)

        def maxes(u):
            k, t, hh, g, k0, n = AU[u]
            v.wait_ge(e("scored"), u + 1)
            s = 2 * (u % 2)
            if k == 0:
                if u:
                    v.wait_ge(e("p_exp"), u - 16)
                sc = SC.rearrange("p (h c) -> p h c", c=64)
                src = ps[:, s, :].rearrange("p (h c) -> p h c", c=64)
                st(tt(sc, src, bc(CC[:, 1024 + 64 * t:1088 + 64 * t].unsqueeze(1), [P, 8, 64]), ADD))
                st(V.reduce_max(CW[:, 0:8], sc, AX))
                st(tt(sc, sc, bc(CW[:, 0:8].unsqueeze(2), [P, 8, 64]), SUB), e("nm_ready"))
                return
            flat = ps[:, s:s + 2, :].rearrange("p b c -> p (b c)")
            st(tt(flat[:, P * (n - 1):P * n], flat[:, P * (n - 1):P * n], caus, ADD))
            if k == 2 and t >= 4:
                st(tt(flat[:, 0:P], flat[:, 0:P], edge, ADD))
            nm = NM[:, u % 4:u % 4 + 1]
            st(V.reduce_max(nm, flat[:, 0:P * n], AX))
            st(V.tensor_scalar_mul(nm, nm, -SCALE), e("nm_ready"))

        def tv_out(u):
            n = AU[u][5]
            if n > 4:
                tv.take(v)
                if u >= 2:
                    v.wait_ge(e("pv_done"), u - 1)
                st(cp(PT[:, u % 2, 512:P * n], ps[:, 5, 0:P * (n - 4)]), tv.free)
            if AU[u][0] == 0:
                t = AU[u][1]
                v.wait_ge(e("p_exp"), u + 1)
                st(V.reduce_sum(SM[:, t % 2, 0:8], PR[:, u % 3, 0:512].rearrange("p (h c) -> p h c", c=64), AX))

        def o_out(u):
            k, t, hh, g, k0, n = AU[u]
            if not (k == 0 or (hh == 3 and g == 1)):
                return
            oi = 3 * t + k
            v.wait_ge(e("pv_done"), u + 1)
            w = CW[:, 8:16]
            st(V.reciprocal(w, SM[:, t % 2, 8 * k:8 * k + 8]))
            st(tt(w.rearrange("p (h g) -> p h g", g=2), w.rearrange("p (h g) -> p h g", g=2),
                  G3[:, t, 8 * k:8 * k + 8].rearrange("p (g h) -> p h g", g=2), MUL))
            if k == 0 and t == 0:
                st(ts(w, w, G[:, GRV:GRV + 1], None, MUL))
            bank = 6 + oi % 2
            n = oi - t - 1
            if k and n >= 2:
                v.wait_ge(e("to_added"), n - 1)
            for gg in range(2):
                src = ps[:, bank, :].rearrange("p (a b g d) -> p a b g d", a=2, b=2, g=2)[:, :, :, gg, :]
                wv = w.rearrange("p (a b g) -> p a b g", a=2, b=2)[:, :, :, gg:gg + 1]
                if k == 0:
                    dst = QT[:, 2 * gg:2 * gg + 2, P * t:P * t + P].rearrange("p a (b d) -> p a b d", b=2)
                else:
                    dst = TO[:, n % 2, 256 * gg:256 * gg + 256].rearrange("p (a b d) -> p a b d", a=2, b=2)
                st(tt(dst, src, bc(wv, [P, 2, 2, 64]), MUL), e("o_used") if gg else None)

        maxes(0)
        for u in range(NU + 1):
            if u + 1 < NU:
                maxes(u + 1)
            if u < NU:
                tv_out(u)
            if u >= 1:
                o_out(u - 1)
        v.wait_ge(e("to_added"), 2 * NT)
        st.mark(e("s4_start"))
        v.wait_ge(outs, R["kv_out"])
        for x in range(2):
            v.wait_ge(e("q_exp"), x + 1)
            hm = G[0:64, GHM:GHM + 8].unsqueeze(2)
            st(tt(EXQ.rearrange("p (h d) -> p h d", d=HD), ps[0:64, x, :].rearrange("p (h d) -> p h d", d=HD), bc(hm, [64, 8, HD]), MUL))
            st(V.reduce_sum(QROW[:, x, :].rearrange("p (g d) -> p g d", g=2), EXQ.rearrange("p (g h d) -> p g d h", g=2, h=4), AX), e("q_rows") if x else None)
        v.wait_ge(e("q_cols"), 1)
        st(cp(QBD, ps[:, 2, 0:128].rearrange("p (x c) -> p x c", x=2)))
        st(cp(NKT, ps[:, 2, 128:136]))
        st(V.memset(PCS, 0.0), e("q_bd"))
        dsts = [CMT[:, 0, 1, :], CMT[:, 1, 1, :], KST[:, 512:T]]

        def keys_out(b, i):
            if b and i == 0:
                v.wait_ge(e("s_hid"), b)
            if b and i == 2:
                v.wait_ge(e("s_scored"), b)
            q = sv.take(v)
            st(cp(dsts[i], ps[:, 2 + q, :]), sv.free)

        for i in range(3):
            keys_out(0, i)
        for b in range(NS):
            v.wait_ge(e("s_kcvc"), b + 1)
            st(cp(KCS[:, 0:NCMP], ps[:, 7, 128:128 + NCMP]))
            st(cp(VCS[0:NCMP, :], ps[0:NCMP, 7, 192:320]), e("s_kcvc_ready"))
            if b + 1 < NS:
                keys_out(b + 1, 0)
            v.wait_ge(e("s_cmps"), b + 1)
            if b:
                v.wait_ge(e("s_pt"), b)
            st(V.reduce_max(SM8[:, 0:1], ps[0:8, 7, 320:320 + NCMP], AX))
            st(V.tensor_scalar_mul(SM8[:, 0:1], SM8[:, 0:1], -SCALE), e("s_m0"))
            v.wait_ge(e("s_e0"), b + 1)
            st(V.reciprocal(SM8[:, 3:4], SM8[:, 3:4]))
            st(ts(PCS[:, 1:1 + NCMP], PCS[:, 1:1 + NCMP], SM8[:, 3:4], None, MUL))
            st(V.reduce_sum(SEL[:, 0:16], PCS[:, 1:65].rearrange("p (j f) -> p j f", f=4), AX))
            st(tt(SEL[:, 0:16], SEL[:, 0:16], PCS[:, 0:64].rearrange("p (j f) -> p j f", f=4)[:, :, 0], ADD), e("s_imp_in"))
            if b + 1 < NS:
                keys_out(b + 1, 1)
            v.wait_ge(e("s_imp"), b + 1)
            imp = SEL[:, 16:32]
            st(cp(imp, ps[0:8, 7, 384:400]))
            st(V.tensor_reduce(SEL[:, 32:33], imp[:, 1:15], AX, MIN))
            st(ts(SEL[:, 34:48], imp[:, 1:15], SEL[:, 32:33], None, ALU.is_equal))
            st(tt(SEL[:, 34:48], SEL[:, 34:48], G[0:8, GIO + 1:GIO + 15], MUL))
            st(V.reduce_max(SEL[:, 33:34], SEL[:, 34:48], AX))
            st(ts(SEL[:, 48:64], G[0:8, GIO:GIO + 16], SEL[:, 33:34], NEG, ALU.is_equal, MUL))
            v.wait_ge(e("s_scored"), b + 1)
            for c in range(2):
                st(tt(SRW[:, 512 * c:512 * c + 512].rearrange("p (j k) -> p j k", k=64),
                      ps[0:8, 4 + c, :].rearrange("p (j k) -> p j k", k=64),
                      bc(SEL[:, 48 + 8 * c:56 + 8 * c].unsqueeze(2), [8, 8, 64]), ADD))
            st(cp(SRW[:, 1024:1025], ps[0:8, 7, 400:401]))
            st(V.reduce_max(SM8[:, 1:2], SRW[:, 0:1025], AX))
            st(V.reduce_max(SM8[:, 2:3], ps[0:8, 6, :], AX))
            st(V.tensor_scalar_mul(SM8[:, 1:3], SM8[:, 1:3], -SCALE), e("s_m1"))
            if b + 1 < NS:
                keys_out(b + 1, 2)
            v.wait_ge(e("s_exp"), 2 * b + 2)
            st(V.reciprocal(SM8[:, 4:6], SM8[:, 4:6]))
            st(ts(SRW[:, 0:1025], SRW[:, 0:1025], SM8[:, 4:5], None, MUL))
            st(ts(PW8, PW8, SM8[:, 5:6], None, MUL), e("s_norm"))
            v.wait_ge(e("s_pt"), b + 1)
            st(cp(PTS[0:NCMP, 0:8], ps[0:NCMP, 7, 404:412]))
            st(cp(PTS[:, 8:72], ps[:, 7, 412:476]))
            st(cp(PTS[0:1, 72:80], ps[0:1, 7, 476:484]))
            st(cp(PTS[:, 80:104], ps[:, 7, 484:508]))
            st(cp(PTS[:, 104:112], ps[:, 6, 0:8]), e("s_pts"))
            v.wait_ge(e("s_pv"), b + 1)
            st(cp(OTS[:, :, 8 * b:8 * b + 8], ps[:, 6, 8:32].rearrange("p (x h) -> p x h", x=3)), e("s_ots"))
        pz_free = pz.free
        v.wait_ge(e("cs_cz"), 1)
        st.mark(pz_free)
        for t in range(1, 9):
            v.wait_ge(e("z_sig"), t)
            if t >= 3:
                v.wait_ge(tz.full, t - 2)
            st(tt(YTK[:, (t - 1) % 2, :], SGZ[:, t % 2, :], ps[:, t % 4, :], MUL), pz_free)
            y3 = YTK[:, (t - 1) % 2, :].rearrange("p (a c) -> p a c", a=4)
            st(tt(y3, y3, QT[:, :, P * (t - 1):P * t], MUL), e("yc_tok"))
        v.wait_ge(e("f_psum"), 1)
        hm = G[0:64, GHM:GHM + 8]
        st(tt(CZX.rearrange("p (h d) -> p h d", d=HD), ps[0:64, 6, :].rearrange("p (h d) -> p h d", d=HD), bc(hm.unsqueeze(2), [64, 8, HD]), MUL))
        st(V.reduce_sum(CZ1, CZX.rearrange("p (h d) -> p d h", d=HD), AX), e("f_sbuf"))
        v.wait_ge(e("f_sig"), 1)
        for i in range(3):
            st(ts(OSB[:, i, :], ps[0:64, 7, 32 + P * i:32 + P * i + 64], G[0:64, GGM:GGM + 1], None, MUL))
            st(stt(OSB[:, i, :], in0=ps[0:64, 7, 96 + P * i:160 + P * i], scalar=G[0:64, GGM + 1:GGM + 2], in1=OSB[:, i, :], op0=MUL, op1=ADD))
        v.wait_ge(e("f_sig"), 1)
        cg = CGX.rearrange("p (x h) -> p x h", x=3)
        st(tt(cg, cg, bc(hm.unsqueeze(1), [64, 3, 8]), MUL))
        st(V.reduce_sum(GX, cg, AX))
        st(ts(OSB[:, 0, :], OSB[:, 0, :], GX[:, 0:1], None, MUL))
        for i in (1, 2):
            st(stt(OSB[:, 0, :], in0=OSB[:, i, :], scalar=GX[:, i:i + 1], in1=OSB[:, 0, :], op0=MUL, op1=ADD))
        v.wait_ge(e("f_sig"), 2)
        st(tt(CZ1, CZ1, CZ2, MUL))
        st(tt(CZ1, CZ1, OSB[:, 0, :], MUL))
        st(tt(YSM.rearrange("p (h d) -> p h d", d=HD), bc(CZ1.unsqueeze(1), [64, 8, HD]), bc(hm.unsqueeze(2), [64, 8, HD]), MUL), e("f_sbuf"))
        v.wait_ge(e("f_psum"), 2)
        v.wait_ge(tz.free, 8)
        st(cp(YF[:, :, 0:8], ps[:, 7, 416:448].rearrange("p (c b) -> p c b", c=4)), e("yc_done"))

        v.wait_ge(ld["cc"], 48)
        v.wait_ge(spilled, 16)
        st(cp(LM, CA[:, 0:1024].rearrange("p (l t) -> p l t", l=8)))
        st(cp(RM, CA[:, 1024:2048]))
        st(cp(ONES, CA[:, 2048:2176]), e("a_start"))

        def a_group(h, i):
            S = AS[h % 2]
            c = i % 3
            cc = slice(CH * c, CH * c + CH)
            if i < 3 or i >= 9:
                n = 6 * h + (i if i < 3 else i - 6)
                v.wait_ge(e("sg_ready"), n + 1)
                st(tt(S["q" if i < 3 else "z"][:, cc], SGA[:, cc], ps[:, n % 2, 0:CH], MUL), pq.free)
            if i == 5:
                v.wait_ge(e("sp_ready"), h + 1)
                st(stt(S["b"], in0=S["b"], scalar=0.0, in1=SGA, op0=MIN, op1=SUB), e("a_lf"))
                st(V.tensor_tensor_scan(S["b"][:, NS:TC], RM, S["b"][:, NS:TC], 0.0, MUL, ADD), e("a_scan"))

        def a_factors(h, q):
            S = AS[h % 2]
            qq = 4 * h + q
            c0 = NS + XR * q
            if qq >= 2:
                v.wait_ge(e("chunk_full"), 2 * (qq - 1))
            for i in range(9):
                x = XQ[:, qq % 2, i, :]
                if i == 7:
                    v.wait_ge(e("eb_ready"), qq + 1)
                    st(tt(x, x, S["q"][:, c0:c0 + XR], MUL))
                    continue
                kk = qq * 8 + (i if i < 7 else 7)
                v.wait_ge(e("d_exp"), kk + 1)
                if i < 7:
                    m = LEVELS[i]
                    def r4(y):
                        return y.rearrange("p (n two m) -> p n two m", two=2, m=m)
                    ev_, xv = r4(DD[:, kk % 2]), r4(x)
                    kv_, qv = r4(S["k"][:, c0:c0 + XR]), r4(S["q"][:, c0:c0 + XR])
                    tt(xv[:, :, 0, :], kv_[:, :, 0, :], ev_[:, :, 0, :], MUL)
                    st(tt(xv[:, :, 1, :], qv[:, :, 1, :], ev_[:, :, 1, :], MUL), e("d_used"))
                else:
                    st(tt(x, S["k"][:, c0:c0 + XR], DD[:, kk % 2], MUL), e("d_used"))
            st.mark(e("x_ready"))

        natt = [0]

        def a_att(h, c):
            natt[0] += 1
            i = 8 * h + c
            v.wait_ge(e("att_full"), natt[0])
            st(tt(MSK, ps[:, 5:7, :].rearrange("p b (l t) -> p (b l) t", t=P), LM, MUL), e("att_masked"))
            if i >= 2:
                v.wait_ge(e("chunk_full"), i - 1)
            st(V.reduce_sum(ATT[:, i % 2], MSK.rearrange("p l t -> p t l"), AX), e("att_ready"))

        def a_chunk(h, c):
            i = 8 * h + c
            v.wait_ge(e("chunk_full"), i + 1)
            if c == 0 and h:
                v.wait_ge(e("a_free"), h)
            st(cp(OT[:, NS + P * c:NS + P * c + P], ps[:, 7, P:2 * P]))
            if c == 0:
                st(cp(STA, ps[:, 7, 2 * P:3 * P]), e("s_ready"))
            else:
                st(stt(STA, in0=STA, scalar=EL[:, (4 * h + c // 2) % 2, c % 2:c % 2 + 1], in1=ps[:, 7, 2 * P:3 * P], op0=MUL, op1=ADD), e("s_ready"))

        def a_sample(h):
            S = AS[h % 2]
            st(ts(LN[:, 0:8], S["k"][:, 0:8], -1.0, 1.0, MUL, ADD))
            v.wait_ge(ld["sts"], 16 * (h + 1))
            st(tt(STS, STS, bc(LN[:, 0:8].unsqueeze(2), [P, 8, P]), MUL))
            natt[0] += 1
            v.wait_ge(e("att_full"), natt[0])
            st(tt(MSK, ps[:, 5:7, :].rearrange("p b (l t) -> p (b l) t", t=P), bc(S["k"][:, 0:8].unsqueeze(2), [P, 8, P]), MUL), e("att_masked"))
            st(tt(STS, STS, MSK, ADD), e("sts_done"))
            v.wait_ge(e("os_full"), h + 1)
            st(cp(OT[:, 0:8], ps[:, 7, 384:392]), e("os_read"))

        def a_norm(h):
            v.wait_ge(e("sq_ready"), h + 1)
            st(stt(OT, in0=OT, scalar=PRM[:, 24 + h:25 + h], in1=AS[h % 2]["z"], op0=MUL, op1=MUL))
            v.wait_ge(e("rms_ready"), h + 1)
            st(tt(YA, OT, SGA, MUL), e("ya_done"))

        for h in range(5):
            for kind, i in a_items(h):
                if kind == "P":
                    a_group(h, i)
                elif kind == "F":
                    a_factors(h - 1, 0)
                elif kind == "S":
                    a_sample(h - 1)
                elif kind == "R":
                    a_att(h - 1, i)
                    if i:
                        a_chunk(h - 1, i - 1)
                    if i % 2 == 0 and i < 6:
                        a_factors(h - 1, i // 2 + 1)
                    if i == 7:
                        a_chunk(h - 1, 7)
                        st.mark(e("ot_ready"))
                elif kind == "N":
                    a_norm(h - 1)

        v.wait_ge(e("a_free"), 4)
        st(V.memset(BXP[:, :, 8:11], 0.0))

        def b_conv(j):
            s = j % 2
            cw = [PRM[:, 28 + 4 * i + j:29 + 4 * i + j] for i in range(4)]
            cb = PRM[:, 44 + j:45 + j]
            v.wait_ge(e("bx_ready"), j + 1)
            xp, us, up = BXP[:, s, 8:11 + T], BU[:, s, 0:NS], BU[:, s, NS:TC]
            st(ts(up, xp[:, 0:T], cw[0], cb, MUL, ADD))
            for i in (1, 2, 3):
                st(stt(up, in0=xp[:, i:i + T], scalar=cw[i], in1=up, op0=MUL, op1=ADD))
            c0 = CST[:, j, 0:24].rearrange("p (b w) -> p b w", w=3)
            st(ts(us, BXP[:, s, 0:8], cw[3], cb, MUL, ADD))
            for i in range(3):
                st(stt(us, in0=c0[:, :, i], scalar=cw[i], in1=us, op0=MUL, op1=ADD), e("u_ready") if i == 2 else None)

        def b_rows(j):
            v.wait_ge(e("oc_rows"), j + 1)
            st(cp(OCR[0:20, j], ps[0:20, 6, P * j:P * j + P]))

        def b_recurrence(j):
            s = j % 2
            v.wait_ge(e("b_at"), j + 1)
            st(tt(BT, BT, BR, MUL), e("b_om"))
            st(tt(BI, BI, BU[:, s], MUL))
            st(tt(BHS[:, 0:NS], BA[:, 0:NS], CST[:, j, 24:32], MUL))
            v.wait_ge(e("b_sq"), j + 1)
            st(tt(BI, BI, BT, MUL))
            st(tt(BHS[:, 0:NS], BHS[:, 0:NS], BI[:, 0:NS], ADD))
            st(V.tensor_tensor_scan(BHS[:, NS:TC], BA[:, NS:TC], BI[:, NS:TC], 0.0, MUL, ADD))
            st(tt(BZ[:, s], BZ[:, s], BR, MUL))
            st(tt(BA, BHS, BZ[:, s], MUL))
            st(cp(YH[0][:, j], BA))
            st(tt(YH[1][:, j], BA, YH[0][:, j].bitcast(F32), SUB))
            oc = OCO[:, s]
            st(cp(oc[:, 0:8], BXP[:, s, 0:8]))
            st(cp(oc[:, 8:11], BXP[:, s, 8 + T:11 + T]))
            st(cp(oc[:, 11:12], BHS[:, TC - 1:TC]))
            st(cp(oc[:, 12:20], BHS[:, 0:8]))
            if j:
                b_rows(j - 1)
            st.mark(e("oc_cols"))
            st.mark(e("b_done"))

        b_conv(0)
        for j in range(4):
            if j < 3:
                b_conv(j + 1)
            b_recurrence(j)
        b_rows(3)
        st.mark(e("oc_done"))
        st.mark(e("y_split"))
        tv.restart_emptying(4)
        n = 0
        for m in range(3):
            if m:
                v.wait_ge(e("y_used"), m)
                for hf in range(2):
                    v.wait_ge(ld["yst"], 16 * (2 * (m - 1) + hf + 1))
                    for i in range(2):
                        src = YST[:, TC * i:TC * i + TC]
                        st(cp(YH[0][:, 2 * hf + i], src))
                        st(tt(YH[1][:, 2 * hf + i], src, YH[0][:, 2 * hf + i].bitcast(F32), SUB))
                    st.mark(e("yst_used"))
                st.mark(e("y_split"))
            for dt in range(8):
                v.wait_ge(e("sgm_ready"), n + 1)
                for c in range(3):
                    b = tv.take(v)
                    cc = slice(CH * c, CH * c + CH)
                    src = ps[:, 4 + b, 0:CH]
                    if m == 0:
                        st(tt(ACC[:, dt, cc], SGM[:, n % 2, cc], src, MUL), tv.free)
                    else:
                        st(tt(TMM, SGM[:, n % 2, cc], src, MUL), tv.free)
                        st(tt(ACC[:, dt, cc], ACC[:, dt, cc], TMM, ADD))
                st.mark(e("sg_used"))
                n += 1
        v.wait_ge(e("y_used"), 3)
        for d in range(8):
            st(cp(H[0][:, d], ACC[:, d]))
            st(tt(H[1][:, d], ACC[:, d], Hf[0][:, d], SUB))
        st.mark(e("acc_split"))
        v.wait_ge(e("gate_psum"), 1)
        st(cp(GSR, ps[0:9, 6:8, :].rearrange("p b c -> p (b c)")), e("gate_sbuf"))
        v.wait_ge(e("gate_psum"), 2)
        st(cp(GB, ps[:, 4:6, :].rearrange("p b c -> p (b c)")), e("gate_sbuf"))
        v.wait_ge(ld["lng"], 32)
        tv.restart_emptying(4)
        for t in range(9):
            r = P if t else NS
            gate = GB if t else GSR[0:8]
            rr, yy, xx = RR[0:r, t % 2], YY[0:r, t % 2], XRL[0:r, t % 3]
            for q in range(2):
                b = tv.take(v)
                st(tt(rr[:, 512 * q:512 * q + 512], gate[:, 512 * q:512 * q + 512], ps[0:r, b, :], MUL), tv.free)
            v.wait_ge(adw_in[t % 3], 48 + 16 * (t // 3 + 1))
            st(stt(rr, in0=xx, scalar=ALPHA, in1=rr, op0=MUL, op1=ADD), e("x_used"))
            for q in range(2):
                st(V.bn_stats(BST[0:r, q], rr[:, 512 * q:512 * q + 512]))
            if t == 0:
                st(V.memset(BAG, 1.0))
            st(V.bn_aggr(BAG[0:r, 0:2], BST[0:r]), e("var_ready"))
            v.wait_ge(e("sd_ready"), t + 1)
            st(V.reciprocal(BAG[0:r, 2:3], LN[0:r, 8 + t % 2:9 + t % 2]))
            if t >= 2:
                v.wait_ge(y_sent[t % 2], 16 * (t // 2))
            st(ts(yy, rr, BAG[0:r, 0:1], BAG[0:r, 2:3], SUB, MUL))
            st(tt(yy, yy, LNG[0:r], MUL))
            st(tt(yy, yy, LNB[0:r], ADD), e("y_ready"))


_INS = ["x_prompt", "x_sample", "c_prompt", "c_sample", "cache_nsa_kv", "page_table", "state_win_kv", "state_hgrn",
        "state_rglru", "state_conv", "ada_w", "ada_b", "w_in", "a_norm_g", "b_conv_w", "b_conv_b", "b_gate_a_w",
        "b_gate_a_b", "b_gate_x_w", "b_gate_x_b", "b_lambda", "c_cmp_pos", "c_cmp_w1", "c_cmp_w2", "w_branch",
        "w_out", "ln_g", "ln_b"]
_OUTS = [("y_prompt", (1, T, D)), ("y_sample", (NS, 1, D)), ("nsa_kv_prompt", (1, 1, T, 4, 2, HD)),
         ("nsa_kv_sample", (1, NS, 1, 4, 2, HD)), ("win_kv_prompt", (1, 1, 512, 2, 2, HD)),
         ("win_kv_sample", (1, NS, 512, 2, 2, HD)), ("hgrn_prompt", (1, 1, 4, P, P)), ("hgrn_sample", (1, NS, 4, P, P)),
         ("rglru_prompt", (1, 1, W)), ("rglru_sample", (1, NS, W)), ("conv_prompt", (1, 1, 3, W)),
         ("conv_sample", (1, NS, 3, W))]


def kernel(**inputs):
    import numpy as np
    from contextlib import ExitStack
    import concourse.bacc as bacc
    from concourse.bass_utils import run_bass_kernel_spmd

    nc = bacc.Bacc("TRN2", target_bir_lowering=False, num_devices=1)
    arrays, ins, outs = {}, {}, {}
    given = {n: np.ascontiguousarray(inputs[n]) for n in _INS}
    for n, x in zip(("const_g", "const_c", "const_a"), constants()):
        given[n] = x
    for n, x in given.items():
        arrays["in_" + n] = x
        ins[n] = nc.dram_tensor("in_" + n, x.shape, mybir.dt.from_np(x.dtype), kind="ExternalInput").ap()
    for n, shape in _OUTS:
        outs[n] = nc.dram_tensor("out_" + n, shape, F32, kind="ExternalOutput").ap()
    with ExitStack() as ctx:
        layer_program(nc, ctx, ins, outs)
    r = run_bass_kernel_spmd(nc, [arrays], core_ids=[0])
    return tuple(r.results[0]["out_" + n] for n, _ in _OUTS)
```
